# Optimizing a Trainium2 kernel written in Bass

```python
import math
import jax, jax.numpy as jnp
from jax import lax
import numpy as np

D_MODEL = 1024
BATCH = 1
SEQ = 2048
DEPTH = 1

HEAD_DIM = 64
N_HEADS_A = 8
N_HEADS_B = 8
WIDTH_A = N_HEADS_A * HEAD_DIM
WIDTH_B = N_HEADS_B * HEAD_DIM
MIX_WIDTH = WIDTH_A + WIDTH_B
IN_SIZES = (WIDTH_A, WIDTH_A, WIDTH_A, WIDTH_B, WIDTH_B, WIDTH_B, MIX_WIDTH)
IN_COLS = sum(IN_SIZES)
DILATED_CONFIGS = ((128, 1), (512, 4), (2048, 16))
BLK = 128
N_BUCKETS = 32
MAX_DISTANCE = 2048
LN_EPS = 1e-5
DEEPNORM_ALPHA = (2.0 * DEPTH) ** 0.25
DEEPNORM_BETA = (8.0 * DEPTH) ** -0.25

kernel_name = "hybrid_dilated_stickbreaking_deepnorm"

def layer_norm(x, g, b):
    xf = x.astype(jnp.float32)
    mu = jnp.mean(xf, axis=-1, keepdims=True)
    var = jnp.mean(jnp.square(xf - mu), axis=-1, keepdims=True)
    y = (xf - mu) * lax.rsqrt(var + LN_EPS) * g.astype(jnp.float32) + b.astype(jnp.float32)
    return y.astype(x.dtype)

def t5_bucket(dist):
    max_exact = N_BUCKETS // 2
    n = np.maximum(dist, 1).astype(np.float32)
    large = max_exact + (np.log(n / max_exact) / math.log(MAX_DISTANCE / max_exact)
                         * (N_BUCKETS - max_exact)).astype(np.int32)
    large = np.minimum(large, N_BUCKETS - 1)
    return np.where(dist < max_exact, dist, large).astype(np.int32)

def dilated_branch(q, k, v, rel_bias, window, dil):
    b, t, h, dh = q.shape
    wc = window // dil
    tc = t // dil
    nb = -(-tc // BLK)
    pad = nb * BLK - tc

    def fold(a):
        a = a.reshape(b, tc, dil, h, dh).transpose(0, 2, 1, 3, 4)
        a = jnp.pad(a, ((0, 0), (0, 0), (0, pad), (0, 0), (0, 0)))
        return a.reshape(b, dil, nb, BLK, h, dh)

    def with_prev(a):
        prev = jnp.pad(a[:, :, :-1], ((0, 0), (0, 0), (1, 0), (0, 0), (0, 0), (0, 0)))
        return jnp.concatenate([prev, a], axis=3)

    def unfold(a):
        trailing = a.shape[4:]
        a = a.reshape((b, dil, nb * BLK) + trailing)[:, :, :tc]
        return jnp.swapaxes(a, 1, 2).reshape((b, t) + trailing)

    qf = fold(q)
    kf = with_prev(fold(k))
    vf = with_prev(fold(v))

    i = np.arange(BLK)[:, None]
    j = np.arange(2 * BLK)[None, :]
    delta = BLK + i - j
    band = (delta >= 0) & (delta <= wc)
    valid = band[None] & ((np.arange(nb)[:, None, None] > 0) | (j[None] >= BLK))
    bucket = t5_bucket(np.clip(delta, 0, wc) * dil)
    bias = jnp.transpose(rel_bias[bucket], (2, 0, 1)).astype(jnp.float32)

    s = jnp.einsum('brnqhd,brnkhd->brnhqk', qf, kf).astype(jnp.float32) / math.sqrt(dh) + bias
    s = jnp.where(valid[:, None], s, -jnp.inf)
    m = jnp.max(s, axis=-1, keepdims=True)
    p = jnp.exp(s - m)
    den = jnp.sum(p, axis=-1)
    o = jnp.einsum('brnhqk,brnkhd->brnqhd', p.astype(v.dtype), vf).astype(jnp.float32)
    o = o / jnp.swapaxes(den, -1, -2)[..., None]
    lse = jnp.swapaxes(m[..., 0] + jnp.log(den), -1, -2)
    return unfold(o), unfold(lse)

def dilated_mixture(q, k, v, rel_bias):
    outs, lses = [], []
    for window, dil in DILATED_CONFIGS:
        o, lse = dilated_branch(q, k, v, rel_bias, window, dil)
        outs.append(o)
        lses.append(lse)
    w = jax.nn.softmax(jnp.stack(lses, axis=0), axis=0)
    y = jnp.sum(w[..., None] * jnp.stack(outs, axis=0), axis=0)
    return y.astype(q.dtype)

def stick_breaking(q, k, v):
    b, t, h, dh = q.shape
    nb = t // BLK
    qb = q.reshape(b, nb, BLK, h, dh).transpose(1, 0, 2, 3, 4)
    starts = jnp.arange(nb, dtype=jnp.int32) * BLK
    kpos = jnp.arange(t, dtype=jnp.int32)
    scale = 1.0 / math.sqrt(dh)

    def one_block(args):
        qblk, start = args
        z = jnp.einsum('bqhd,bkhd->bhqk', qblk, k).astype(jnp.float32) * scale
        qpos = start + jnp.arange(BLK, dtype=jnp.int32)
        causal = kpos[None, :] < qpos[:, None]
        log_beta = jax.nn.log_sigmoid(z)
        log1m = jnp.where(causal, jax.nn.log_sigmoid(-z), 0.0)
        after = lax.cumsum(log1m, axis=3, reverse=True) - log1m
        a = jnp.where(causal, jnp.exp(log_beta + after), 0.0)
        return jnp.einsum('bhqk,bkhd->bqhd', a.astype(v.dtype), v)

    out = lax.map(one_block, (qb, starts))
    return out.transpose(1, 0, 2, 3, 4).reshape(b, t, h, dh)

def setup_inputs(seed: int = 0) -> dict:
    key = jax.random.key(seed)
    ks = jax.random.split(key, 10)
    x = jax.random.normal(ks[0], (BATCH, SEQ, D_MODEL), jnp.float32)
    ln0_g = 1.0 + 0.02 * jax.random.normal(ks[1], (D_MODEL,), jnp.float32)
    ln0_b = 0.02 * jax.random.normal(ks[2], (D_MODEL,), jnp.float32)
    col_scale = np.ones((IN_COLS,), np.float32)
    offs = np.concatenate([[0], np.cumsum(IN_SIZES)])
    col_scale[offs[2]:offs[3]] = DEEPNORM_BETA
    col_scale[offs[5]:offs[6]] = DEEPNORM_BETA
    w_in = (jax.random.normal(ks[3], (DEPTH, D_MODEL, IN_COLS), jnp.float32)
            * (D_MODEL ** -0.5) * jnp.asarray(col_scale))
    w_out = (jax.random.normal(ks[4], (DEPTH, MIX_WIDTH, D_MODEL), jnp.float32)
             * (MIX_WIDTH ** -0.5) * DEEPNORM_BETA)
    b_out = 0.02 * jax.random.normal(ks[5], (DEPTH, D_MODEL), jnp.float32)
    ln_g = 1.0 + 0.02 * jax.random.normal(ks[6], (DEPTH, D_MODEL), jnp.float32)
    ln_b = 0.02 * jax.random.normal(ks[7], (DEPTH, D_MODEL), jnp.float32)
    rel_bias = 0.5 * jax.random.normal(ks[8], (N_BUCKETS, N_HEADS_A), jnp.float32)
    return {"x": x, "ln0_g": ln0_g, "ln0_b": ln0_b, "w_in": w_in, "w_out": w_out,
            "b_out": b_out, "ln_g": ln_g, "ln_b": ln_b, "rel_bias": rel_bias}

def reference(x, ln0_g, ln0_b, w_in, w_out, b_out, ln_g, ln_b, rel_bias):
    b, t, _ = x.shape
    split_at = [int(s) for s in np.cumsum(IN_SIZES)[:-1]]
    h = layer_norm(x, ln0_g, ln0_b)
    for l in range(DEPTH):
        proj = jnp.einsum('btd,dc->btc', h, w_in[l])
        qa, ka, va, qb, kb, vb, gate = jnp.split(proj, split_at, axis=-1)
        heads_a = lambda a: a.reshape(b, t, N_HEADS_A, HEAD_DIM)
        heads_b = lambda a: a.reshape(b, t, N_HEADS_B, HEAD_DIM)
        ya = dilated_mixture(heads_a(qa), heads_a(ka), heads_a(va), rel_bias).reshape(b, t, WIDTH_A)
        yb = stick_breaking(heads_b(qb), heads_b(kb), heads_b(vb)).reshape(b, t, WIDTH_B)
        y = jnp.concatenate([ya, yb], axis=-1) * jax.nn.silu(gate)
        out = jnp.einsum('btc,cd->btd', y, w_out[l]) + b_out[l]
        h = layer_norm(DEEPNORM_ALPHA * h + out, ln_g[l], ln_b[l])
    return h


_drawn_inputs = setup_inputs


def setup_inputs(seed=0):
    import zlib

    import numpy as np

    out = dict(_drawn_inputs(seed))
    spreads = {}
    factors = {'ln0_b': 2.73, 'b_out': 3.228, 'ln_g': 2.74, 'ln_b': 2.868, 'rel_bias': 8.0}
    for name, (base, spread) in spreads.items():
        noise = np.random.default_rng([zlib.crc32(name.encode()), seed]).standard_normal(out[name].shape)
        drawn = base * np.exp(spread * noise) if base else spread * noise
        out[name] = __import__('jax').numpy.asarray(drawn.astype(out[name].dtype))
    for name, factor in factors.items():
        out[name] = (out[name] * factor).astype(out[name].dtype)
    return out
```

```python
from contextlib import ExitStack

import numpy as np

import concourse.bass as bass
from concourse import mybir

F32 = mybir.dt.float32
F32R = mybir.dt.float32r
ALU = mybir.AluOpType
ACT = mybir.ActivationFunctionType

T = 2048
D = 1024
DH = 64
HEADS = 8
WIDTH = HEADS * DH
IN_COLS = 6 * WIDTH + 2 * WIDTH
GATE_COL = 6 * WIDTH
P = 128
KD = D // P
TB = T // P
CH = 512
NCH = T // CH
QB = CH // P
DILATIONS = (1, 4, 16)
BAND = 128
N_BUCKETS = 32
MAX_DISTANCE = 2048
TOE = 3 * P
MASKED = -1e30
EPS = 1e-5
ALPHA = 2.0 ** 0.25
SCALE = DH ** -0.5
ROW = DH + 2


def at(it, per_turn, n):
    return it * per_turn + n


def bucket_onehot():
    oh = np.zeros((N_BUCKETS + 1, 3, TOE), np.float32)
    max_exact = N_BUCKETS // 2
    for c, dil in enumerate(DILATIONS):
        for u in range(TOE):
            delta = 2 * P - 1 - u
            if 0 <= delta <= BAND:
                dist = delta * dil
                if dist < max_exact:
                    b = dist
                else:
                    n = np.float32(dist)
                    b = max_exact + int(np.float32(np.log(n / np.float32(max_exact))
                                                   / np.log(MAX_DISTANCE / max_exact)
                                                   * (N_BUCKETS - max_exact)))
                    b = min(b, N_BUCKETS - 1)
                oh[b, c, u] = 1.0
            else:
                oh[N_BUCKETS, c, u] = 1.0
    return oh.reshape(N_BUCKETS + 1, 3 * TOE)


def block_selector():
    sel = np.zeros((TB, T), np.float32)
    for b in range(TB):
        sel[b, b * P:(b + 1) * P] = 1.0
    return sel


def stick_mask():
    m = np.zeros((P, CH), np.float32)
    for q in range(P):
        m[q, CH - P + q:] = 1.0
    return m


class Memory:

    def __init__(self, nc, stack):
        self.nc, self.stack = nc, stack

    def sb(self, name, shape, dtype=F32):
        return self.stack.enter_context(self.nc.sbuf_tensor(name, shape, dtype))

    def ps(self, name, shape=(P, CH)):
        return self.stack.enter_context(self.nc.psum_tensor(name, list(shape), F32))

    def ring(self, name, n, shape, dtype=F32):
        return [self.sb(f"{name}{i}", shape, dtype) for i in range(n)]

    def banks(self, name, n):
        return [self.ps(f"{name}{i}") for i in range(n)]

    def sems(self, name, n):
        return [self.sem(f"{name}{i}") for i in range(n)]

    def sem(self, name):
        return self.stack.enter_context(self.nc.semaphore(name))


def norm_phase(nc, x, ln_g, ln_b, rel_bias, onehot, xhat_d, toe_d, ident, h_hi, h_lo):
    GROUPS = 2
    TILES = 4 * GROUPS
    TURNS = TB // TILES
    with ExitStack() as stack:
        m = Memory(nc, stack)
        x_sb = m.ring("x_sb", 4, [P, D])
        xh_sb = m.ring("xh_sb", TILES, [P, D])
        h_full = m.ring("h_full", 2, [P, CH])
        stats = m.ring("stats", 2, [P, 12])
        mv = m.ring("mv", 2, [P, 2])
        rstd = m.ring("rstd", 2, [P, 1])
        neg_half = m.sb("neg_half", [P, 1])
        g_col = m.sb("g_col", [P, KD])
        b_col = m.sb("b_col", [P, KD])
        rb = m.sb("rb", [N_BUCKETS + 1, HEADS])
        oh = m.sb("oh", [N_BUCKETS + 1, 3 * TOE])
        toe = m.sb("toe", [HEADS, 3, TOE])
        tp = m.banks("ln_tp", 4)
        toe_ps = m.banks("toe_ps", 3)
        x_loaded = m.sems("x_loaded", 4)
        xh_stored = m.sems("xh_stored", TILES)
        col_loaded, rb_loaded = m.sem("col_loaded"), m.sem("rb_loaded")
        ident_step, rb_set, stats_done = m.sem("ident_step"), m.sem("rb_set"), m.sem("stats_done")
        mv_done, var_done, rstd_done = m.sem("mv_done"), m.sem("var_done"), m.sem("rstd_done")
        xh_done, tp_done = m.sem("xh_done"), m.sem("tp_done")
        full_done, hi_done, lo_done = m.sem("full_done"), m.sem("h_hi_done"), m.sem("h_lo_done")
        passed, pool_passed = m.sem("passed"), m.sem("pool_passed")
        toe_mm, toe_ready, toe_stored = m.sem("toe_mm"), m.sem("toe_ready"), m.sem("toe_stored")
        block = stack.enter_context(nc.Block())

        @block.sync
        def _(sp):
            sp.wait_ge(rb_set, 1)
            sp.dma_start(rb[0:N_BUCKETS, :], rel_bias).then_inc(rb_loaded, 16)
            sp.dma_start(oh[:], onehot).then_inc(rb_loaded, 16)
            with sp.Fori(0, TURNS) as it:
                for n in range(TILES):
                    sp.wait_ge(xh_done, at(it, TILES, n + 1))
                    sp.dma_start(x_sb[n % 4][:], x[bass.ds(at(it, TILES, n) * P, P), :]) \
                        .then_inc(x_loaded[n % 4], 16)

        @block.gpsimd
        def _(pool):
            pool.memset(rb[:], MASKED).then_inc(rb_set, 1)
            pool.memset(neg_half[:], -0.5).then_inc(rb_set, 1)
            pool.memset(ident[:], 0.0).then_inc(ident_step, 1)
            pool.wait_ge(ident_step, 1)
            pool.affine_select(out=ident[:], in_=ident[:], compare_op=ALU.not_equal, fill=1.0,
                               base=0, pattern=[[-1, P]], channel_multiplier=1) \
                .then_inc(ident_step, 1)
            pool.wait_ge(rb_set, 2)
            with pool.Fori(0, TURNS) as it:
                for n in range(TILES):
                    pool.wait_ge(mv_done, at(it, TILES, n + 1))
                    pool.sem_inc(pool_passed, 1)
                    pool.tensor_scalar(rstd[n % 2][:], mv[n % 2][:, 1:2], EPS, None, ALU.add) \
                        .then_inc(var_done, 1)
                    pool.wait_ge(var_done, at(it, TILES, n + 1))
                    pool.tensor_tensor(rstd[n % 2][:], rstd[n % 2][:], neg_half[:], ALU.pow) \
                        .then_inc(rstd_done, 1)

        @block.vector
        def _(dve):
            dve.sem_inc(xh_done, 4)

            def normalise(it, n):
                dve.wait_ge(rstd_done, at(it, TILES, n + 1))
                dve.wait_ge(xh_stored[n], at(it, 16, 16))
                dve.wait_ge(tp_done, at(it, KD * GROUPS, KD * (n // 4 + 1)))
                dve.tensor_scalar(xh_sb[n][:], x_sb[n % 4][:], mv[n % 2][:, 0:1],
                                  rstd[n % 2][:], ALU.subtract, ALU.mult).then_inc(xh_done, 1)

            def low_parts(it, g):
                for k in range(KD):
                    step = g * KD + k
                    cols = bass.ds((at(it, GROUPS, g)) * CH, CH)
                    dve.wait_ge(hi_done, at(it, KD * GROUPS, step + 1))
                    dve.tensor_tensor(h_lo[:, k, cols], h_full[step % 2][:],
                                      h_hi[:, k, cols].bitcast(F32), ALU.subtract) \
                        .then_inc(lo_done, 1)

            with dve.Fori(0, TURNS) as it:
                for n in range(TILES):
                    dve.wait_ge(x_loaded[n % 4], at(it, 16 * GROUPS, 16 * (n // 4 + 1)))
                    for half in range(2):
                        last = dve.bn_stats(stats[n % 2][:, 6 * half:6 * half + 6],
                                            x_sb[n % 4][:, half * CH:(half + 1) * CH])
                    last.then_inc(stats_done, 1)
                    dve.wait_ge(stats_done, at(it, TILES, n + 1))
                    dve.sem_inc(passed, 1)
                    dve.bn_aggr(mv[n % 2][:], stats[n % 2][:]).then_inc(mv_done, 1)
                    if n >= 1:
                        normalise(it, n - 1)
                    if n == 6:
                        low_parts(it, 0)
                normalise(it, TILES - 1)
                low_parts(it, 1)

        @block.tensor
        def _(pe):
            pe.wait_ge(rb_loaded, 32)
            for c in range(3):
                last = pe.matmul(toe_ps[c][0:HEADS, 0:TOE], rb[:], oh[:, c * TOE:(c + 1) * TOE],
                                 start=True, stop=True)
            last.then_inc(toe_mm, 1)
            pe.wait_ge(ident_step, 2)
            pe.sem_inc(tp_done, KD * GROUPS)
            with pe.Fori(0, TURNS) as it:
                for g in range(GROUPS):
                    pe.wait_ge(xh_done, 4 + at(it, TILES, 4 * (g + 1)))
                    for k in range(KD):
                        step = g * KD + k
                        pe.wait_ge(lo_done, at(it, KD * GROUPS, step + 1))
                        for j in range(4):
                            last = pe.transpose(tp[step % 4][:, j * P:(j + 1) * P],
                                                xh_sb[4 * g + j][:, k * P:(k + 1) * P], ident[:])
                        last.then_inc(tp_done, 1)

        @block.scalar
        def _(act):
            for n in range(TILES):
                act.sem_inc(xh_stored[n], 16)
            act.sem_inc(lo_done, 4)
            with nc.allow_non_contiguous_dma("two short vectors"):
                act.dma_start(g_col[:], ln_g.rearrange("(k p) -> p k", p=P)).then_inc(col_loaded, 16)
                act.dma_start(b_col[:], ln_b.rearrange("(k p) -> p k", p=P)).then_inc(col_loaded, 16)
            act.wait_ge(toe_mm, 1)
            for c in range(3):
                last = act.activation(toe[:, c, :], toe_ps[c][0:HEADS, 0:TOE], ACT.Copy, scale=1.0 / SCALE)
            last.then_inc(toe_ready, 1)
            act.wait_ge(toe_ready, 1)
            for c in range(3):
                act.dma_start(toe_d[c], toe[:, c, :].unsqueeze(1).broadcast_to([HEADS, P, TOE])) \
                    .then_inc(toe_stored, 16)
            act.wait_ge(col_loaded, 32)
            with act.Fori(0, TURNS) as it:
                for g in range(GROUPS):
                    for j in range(4):
                        n = 4 * g + j
                        act.wait_ge(xh_done, 4 + at(it, TILES, n + 1))
                        act.dma_start(xhat_d[bass.ds(at(it, TILES, n) * P, P), :], xh_sb[n][:]) \
                            .then_inc(xh_stored[n], 16)
                    for k in range(KD):
                        step = g * KD + k
                        cols = bass.ds((at(it, GROUPS, g)) * CH, CH)
                        act.wait_ge(tp_done, KD * GROUPS + at(it, KD * GROUPS, step + 1))
                        act.wait_ge(lo_done, 2 + at(it, KD * GROUPS, step + 1))
                        act.activation(h_full[step % 2][:], tp[step % 4][:], ACT.Identity,
                                       scale=g_col[:, k:k + 1], bias=b_col[:, k:k + 1])
                        act.activation(h_hi[:, k, cols], tp[step % 4][:], ACT.Identity,
                                       scale=g_col[:, k:k + 1], bias=b_col[:, k:k + 1]) \
                            .then_inc(hi_done, 1)
            act.wait_ge(toe_stored, 48)
            for n in range(TILES):
                act.wait_ge(xh_stored[n], 16 + 16 * TURNS)


SEGMENTS = (("qk", 0, 0, 8), ("qk", 3 * WIDTH, 2 * WIDTH, 8), ("gate", GATE_COL, 0, 8),
            ("va", 2 * WIDTH, 0, 4), ("vb", 5 * WIDTH, 0, 4))
W_TILES = sum(s[3] for s in SEGMENTS)


def segments():
    before = 0
    for kind, _, row, tiles in SEGMENTS:
        yield kind, row, tiles // 2, before
        before += tiles


def projection_phase(nc, w_tiles, qk_hi_d, qk_lo_d, gate_d, va_d, vb_d, ident, h_hi, h_lo):
    TILES = 2
    STEPS = TILES * NCH
    V_TILES = 24
    with ExitStack() as stack:
        m = Memory(nc, stack)
        w_raw = m.ring("w_raw", 2, [P, KD, P])
        w_hi = m.ring("w_hi", 2, [P, KD, P], F32R)
        w_lo = m.ring("w_lo", 2, [P, KD, P], F32R)
        st_hi = m.ring("st_hi", 2, [P, T], F32R)
        st_lo = m.ring("st_lo", 2, [P, T], F32R)
        vt = m.ring("vt", 2, [P, CH])
        zero_row = m.sb("zero_row", [1, WIDTH])
        acc = m.banks("proj", 4)
        vtp = m.banks("vtp", 2)
        w_loaded = m.sems("w_loaded", 2)
        w_hi_done, w_split = m.sem("w_hi_done"), m.sem("w_split")
        proj_done, vt_done, vtp_done = m.sem("proj_done"), m.sem("vt_done"), m.sem("vtp_done")
        first_done, second_done = m.sem("first_done"), m.sem("second_done")
        hi_stored, lo_stored = m.sems("hi_stored", 2), m.sems("lo_stored", 2)
        zero_set, zero_stored = m.sem("zero_set"), m.sem("zero_stored")
        block = stack.enter_context(nc.Block())

        @block.sync
        def _(sp):
            sp.wait_ge(zero_set, 1)
            sp.dma_start(vb_d[0:1, :], zero_row[:]).then_inc(zero_stored, 16)
            with sp.Fori(0, W_TILES // TILES) as it:
                for j in range(TILES):
                    sp.wait_ge(w_split, at(it, TILES, j + 1))
                    sp.dma_start(w_raw[j][:], w_tiles[bass.ds(at(it, TILES, j), 1)]
                                 .rearrange("o p k c -> (o p) k c")).then_inc(w_loaded[j], 16)
            sp.wait_ge(zero_stored, 16)

        @block.gpsimd
        def _(pool):
            pool.memset(zero_row[:], 0.0).then_inc(zero_set, 1)

        @block.tensor
        def _(pe):
            pe.sem_inc(proj_done, 2 * NCH)
            pe.sem_inc(vtp_done, 2)

            def transpose_values(kind, base, it, s):
                step = base + at(it, STEPS, s)
                pe.wait_ge(vt_done, 4 + at(it, STEPS, s + 1) + (base - V_TILES * NCH))
                if kind == "va":
                    pe.wait_ge(second_done, 4 + step - 1)
                else:
                    pe.wait_ge(first_done, step - 1)
                for b in range(4):
                    last = pe.transpose(vtp[s % 2][:, b * P:(b + 1) * P],
                                        vt[s % 2][:, b * P:(b + 1) * P], ident[:])
                last.then_inc(vtp_done, 1)

            for kind, row, turns, before in segments():
                base = before * NCH
                if kind == "vb":
                    pe.wait_ge(second_done, 4 + base)
                if kind == "va":
                    pe.wait_ge(second_done, 4 + base)
                with pe.Fori(0, turns) as it:
                    for s in range(STEPS):
                        j, ch = divmod(s, NCH)
                        if ch == 0:
                            pe.wait_ge(w_split, 2 + before + at(it, TILES, j + 1))
                        if kind in ("qk", "gate"):
                            pe.wait_ge(second_done, base + at(it, STEPS, s + 1))
                        else:
                            pe.wait_ge(vt_done, base - V_TILES * NCH + at(it, STEPS, s + 1))
                        cols = slice(ch * CH, (ch + 1) * CH)
                        passes = [(w, h, k) for k in range(KD)
                                  for w, h in ((w_hi, h_hi), (w_hi, h_lo), (w_lo, h_hi))]
                        for n, (w, h, k) in enumerate(passes):
                            last = pe.matmul(acc[s % 4][:], w[j][:, k, :], h[:, k, cols],
                                             start=(n == 0), stop=(n == len(passes) - 1))
                        last.then_inc(proj_done, 1)
                        if kind in ("va", "vb") and s >= 1:
                            transpose_values(kind, base, it, s - 1)
                    if kind in ("va", "vb"):
                        transpose_values(kind, base, it, STEPS - 1)

        @block.scalar
        def _(act):
            for j in range(TILES):
                act.sem_inc(hi_stored[j], 32)
                act.sem_inc(lo_stored[j], 32)

            def store(kind, row, it, j, steps):
                act.wait_ge(first_done, steps)
                if kind != "vb":
                    act.wait_ge(second_done, 4 + steps)
                rows = bass.ds(at(it, TILES, j) * P + row, P)
                hi, lo = st_hi[j][:].bitcast(F32), st_lo[j][:].bitcast(F32)
                if kind == "qk":
                    act.sem_inc(hi_stored[j], 16)
                    act.sem_inc(lo_stored[j], 16)
                    act.dma_start(qk_hi_d[rows, :], hi).then_inc(hi_stored[j], 16)
                    act.dma_start(qk_lo_d[rows, :], lo).then_inc(lo_stored[j], 16)
                elif kind == "gate":
                    act.sem_inc(hi_stored[j], 32)
                    act.sem_inc(lo_stored[j], 16)
                    act.dma_start(gate_d[rows, :], lo).then_inc(lo_stored[j], 16)
                elif kind == "va":
                    for part, st, stored in ((0, hi, hi_stored[j]), (1, lo, lo_stored[j])):
                        src = st.rearrange("p (b h d) -> p b h d", b=TB, h=2)
                        for hh in range(2):
                            dst = va_d[bass.ds(at(it, 2 * TILES, 2 * j + hh), 1), :, part, :]
                            act.dma_start(dst.rearrange("o (b p) d -> p (o b) d", p=P),
                                          src[:, :, hh, :]).then_inc(stored, 16)
                else:
                    act.sem_inc(hi_stored[j], 16)
                    act.sem_inc(lo_stored[j], 32)
                    dst = vb_d[1:T + 1, bass.ds(at(it, TILES, j) * P, P)]
                    act.dma_start(dst.rearrange("(b p) c -> p b c", p=P),
                                  hi.rearrange("p (b c) -> p b c", b=TB)).then_inc(hi_stored[j], 16)

            for kind, row, turns, before in segments():
                base = before * NCH
                with act.Fori(0, turns) as it:
                    for s in range(STEPS):
                        j, ch = divmod(s, NCH)
                        cols = slice(ch * CH, (ch + 1) * CH)
                        if ch == 0:
                            act.wait_ge(hi_stored[j], 16 * before + at(it, 32, 32))
                        if kind in ("qk", "gate"):
                            act.wait_ge(proj_done, 2 * NCH + base + at(it, STEPS, s + 1))
                        else:
                            act.wait_ge(vtp_done, 2 + base - V_TILES * NCH + at(it, STEPS, s + 1))
                        if kind == "qk":
                            step = act.activation(st_hi[j][:, cols], acc[s % 4][:], ACT.Copy)
                        elif kind == "gate":
                            step = act.activation(st_hi[j][:, cols].bitcast(F32), acc[s % 4][:], ACT.Sigmoid)
                        elif kind == "va":
                            step = act.activation(st_hi[j][:, cols], vtp[s % 2][:], ACT.Copy)
                        else:
                            step = act.activation(st_hi[j][:, cols].bitcast(F32), vtp[s % 2][:], ACT.Copy)
                        step.then_inc(first_done, 1)
                        if s == NCH:
                            store(kind, row, it, 0, base + at(it, STEPS, NCH))
                    store(kind, row, it, 1, base + at(it, STEPS, STEPS))
            for j in range(TILES):
                act.wait_ge(hi_stored[j], 32 + 16 * W_TILES)
                act.wait_ge(lo_stored[j], 32 + 16 * W_TILES)

        @block.vector
        def _(dve):
            dve.sem_inc(w_split, 2)
            dve.sem_inc(second_done, 4)
            dve.sem_inc(vt_done, 4)

            def split_weights(slot, n):
                dve.wait_ge(w_loaded[slot], (n - slot) * 8 + 16)
                dve.wait_ge(proj_done, NCH * (n + 1))
                dve.tensor_copy(w_hi[slot][:], w_raw[slot][:]).then_inc(w_hi_done, 1)
                dve.wait_ge(w_hi_done, n + 1)
                dve.tensor_tensor(w_lo[slot][:], w_raw[slot][:], w_hi[slot][:].bitcast(F32),
                                  ALU.subtract).then_inc(w_split, 1)

            def low_part(base, it, s):
                j, ch = divmod(s, NCH)
                cols = slice(ch * CH, (ch + 1) * CH)
                dve.wait_ge(first_done, base + at(it, STEPS, s + 1))
                dve.tensor_tensor(st_lo[j][:, cols], vtp[s % 2][:], st_hi[j][:, cols].bitcast(F32),
                                  ALU.subtract).then_inc(second_done, 1)

            split_weights(0, 0)
            for kind, row, turns, before in segments():
                base = before * NCH
                def turn(it):
                    for s in range(STEPS):
                        j, ch = divmod(s, NCH)
                        cols = slice(ch * CH, (ch + 1) * CH)
                        step = base + at(it, STEPS, s + 1)
                        if ch == 0:
                            dve.wait_ge(lo_stored[j], 16 * before + at(it, 32, 32))
                        if kind == "qk":
                            dve.wait_ge(first_done, step)
                            dve.tensor_tensor(st_lo[j][:, cols], acc[s % 4][:],
                                              st_hi[j][:, cols].bitcast(F32),
                                              ALU.subtract).then_inc(second_done, 1)
                        elif kind == "gate":
                            dve.wait_ge(first_done, step)
                            dve.tensor_tensor(st_lo[j][:, cols].bitcast(F32), acc[s % 4][:],
                                              st_hi[j][:, cols].bitcast(F32),
                                              ALU.mult).then_inc(second_done, 1)
                        else:
                            dve.wait_ge(proj_done, 2 * NCH + step)
                            dve.wait_ge(vtp_done, step - V_TILES * NCH)
                            dve.tensor_copy(vt[s % 2][:], acc[s % 4][:]).then_inc(vt_done, 1)
                            if kind == "va" and s >= 1:
                                low_part(base, it, s - 1)
                        if ch == 0 and not (kind == "vb" and it == turns - 1 and j == TILES - 1):
                            split_weights(1 - j, before + at(it, TILES, j + 1))
                    if kind == "va":
                        low_part(base, it, STEPS - 1)

                if kind == "vb":
                    for it in range(turns):
                        turn(it)
                else:
                    with dve.Fori(0, turns) as it:
                        turn(it)


class HeadTiles:
    QK_LOADS = 5

    def __init__(self, nc, stack):
        m = Memory(nc, stack)
        self.k_both = m.ring("k_both", 2, [P, T], F32R)
        self.q_hi2 = m.ring("q_hi2", 2, [P, T], F32R)
        self.q_lo0 = m.ring("q_lo0", 2, [P, T], F32R)
        self.bias = m.ring("bias", 2, [P, 3, 2 * P])
        self.qk_loaded, self.bias_loaded = m.sems("a_qk_loaded", 2), m.sems("bias_loaded", 2)

    def qk_pieces(self, qk_hi_d, qk_lo_d, q, k, par, cols=slice(0, T)):
        parts = ((self.k_both, 0, qk_hi_d, k), (self.k_both, DH, qk_lo_d, k),
                 (self.q_hi2, 0, qk_hi_d, q), (self.q_hi2, DH, qk_hi_d, q), (self.q_lo0, 0, qk_lo_d, q))
        return [(tile[par][half:half + DH, cols].bitcast(F32), src[bass.ds(row, DH), cols])
                for tile, half, src, row in parts]

    def load_dilated(self, sp, qk_hi_d, qk_lo_d, toe_d, head, par):
        for dst, src in self.qk_pieces(qk_hi_d, qk_lo_d, head * DH, head * DH + WIDTH, par):
            sp.dma_start(dst, src).then_inc(self.qk_loaded[par], 16)
        for c in range(3):
            flat = toe_d[c, bass.ds(head, 1), :, :].rearrange("o a b -> o (a b)")
            band = flat[:, P - 1:P - 1 + P * (TOE - 1)].rearrange("o (i u) -> (o i) u", u=TOE - 1)
            sp.dma_start(self.bias[par][:, c, :], band[:, 0:2 * P]).then_inc(self.bias_loaded[par], 16)


def stick_phase(nc, heads, qk_hi_d, qk_lo_d, gate_d, vb_d, toe_d, selector, mask, ident, y_d):
    TURN_HEADS = 2
    TURNS = HEADS // TURN_HEADS
    UNITS = [(par, g, c) for par in range(TURN_HEADS) for g in range(NCH) for c in range(g, -1, -1)]
    STEPS = len(UNITS) * QB
    GROUPS = TURN_HEADS * NCH
    W_SLOTS = 16
    TRANSPOSE_LAG, HIGH_LAG, LOW_LAG, VALUES_LAG = 7, 8, 8, 11
    Q_ROW, K_ROW = 2 * WIDTH, 3 * WIDTH
    with ExitStack() as stack:
        m = Memory(nc, stack)
        k_both, q_hi2, q_lo0 = heads.k_both, heads.q_hi2, heads.q_lo0
        v_cur = m.ring("v_cur", 2, [P, TB, DH])
        v_prev = m.ring("v_prev", 2, [P, TB, DH])
        v_diff = m.sb("v_diff", [P, TB, DH])
        dv = m.ring("dv", 2, [P, TB, 2 * DH], F32R)
        v_end = m.ring("v_end", 2, [TB, DH])
        v_end2 = m.ring("v_end2", 2, [TB, 2 * DH], F32R)
        gate = m.ring("gate", 2, [DH, T])
        w = m.ring("w", 4, [P, CH])
        W = m.ring("W", W_SLOTS, [P, CH])
        WT_hi = m.ring("WT_hi", 4, [P, CH], F32R)
        WT_lo = m.ring("WT_lo", 4, [P, CH], F32R)
        o_low = m.ring("o_low", 2, [DH, CH])
        y_sum = m.ring("y_sum", 2, [DH, CH])
        y_out = m.ring("y_out", 2, [DH, CH])
        sel_f = m.sb("sel_f", [TB, T])
        sel = m.sb("sel", [TB, T], F32R)
        zeros = m.sb("zeros", [P, CH])
        ones_above = m.sb("ones_above", [P, CH])
        z_ps, t_ps, o_ps = m.banks("z_ps", 2), m.banks("wt_ps", 4), m.banks("o_ps", 2)
        first_loaded, v_loaded, rest_loaded = (m.sems("b_first_loaded", 2), m.sems("b_v_loaded", 2),
                                               m.sems("b_rest_loaded", 2))
        y_stored = m.sems("b_y_stored", 2)
        sel_loaded, mask_loaded, sel_done = m.sem("sel_loaded"), m.sem("mask_loaded"), m.sem("sel_done")
        zeros_set, pool_zeros_set = m.sem("b_zeros_set"), m.sem("b_pool_zeros_set")
        pool_passed = m.sem("b_pool_passed")
        dv_step, dv_done = m.sem("dv_step"), m.sem("dv_done")
        z_done, w_done, scan_done = m.sem("z_done"), m.sem("w_done"), m.sem("scan_done")
        t_done, hi_done, lo_done = m.sem("wt_done"), m.sem("wt_hi_done"), m.sem("wt_lo_done")
        av_done, low_copied, sum_done, y_done = (m.sem("b_av_done"), m.sem("o_low_copied"),
                                                 m.sem("y_sum_done"), m.sem("b_y_done"))
        QK, V, REST = HeadTiles.QK_LOADS, 3, HeadTiles.QK_LOADS + 1
        block = stack.enter_context(nc.Block())

        def keys(i, g, c):
            return P * (i + 1) if c == g else CH

        def first_block(j, g, c):
            return j if c == g else 0

        def turn_index(u):
            return u * QB

        def group_index(par, g):
            return par * NCH + g

        @block.sync
        def _(sp):
            def load_first(head, par):
                for dst, src in heads.qk_pieces(qk_hi_d, qk_lo_d, head * DH + Q_ROW, head * DH + K_ROW,
                                                par, slice(0, CH)):
                    sp.dma_start(dst, src).then_inc(first_loaded[par], 16)

            def load_rest(head, par):
                for dst, src in ((v_cur[par][:], vb_d[1:T + 1, bass.ds(head * DH, DH)]
                                  .rearrange("(b p) d -> p b d", p=P)),
                                 (v_prev[par][:], vb_d[0:T, bass.ds(head * DH, DH)]
                                  .rearrange("(b p) d -> p b d", p=P)),
                                 (v_end[par][:], vb_d[P:T + 1:P, bass.ds(head * DH, DH)])):
                    sp.dma_start(dst, src).then_inc(v_loaded[par], 16)
                pieces = heads.qk_pieces(qk_hi_d, qk_lo_d, head * DH + Q_ROW, head * DH + K_ROW, par,
                                         slice(CH, T))
                pieces.append((gate[par][:], gate_d[bass.ds(head * DH + WIDTH, DH), :]))
                for dst, src in pieces:
                    sp.dma_start(dst, src).then_inc(rest_loaded[par], 16)

            def store(it, par, g):
                n = group_index(par, g)
                sp.wait_ge(y_done, 2 + at(it, GROUPS, n + 1))
                sp.dma_start(y_d[bass.ds(at(it, TURN_HEADS, par) * DH + WIDTH, DH), g * CH:(g + 1) * CH],
                             y_out[n % 2][:]).then_inc(y_stored[n % 2], 16)

            sp.sem_inc(y_stored[0], 16)
            sp.sem_inc(y_stored[1], 16)
            load_first(0, 0)
            sp.dma_start(ones_above[:], mask).then_inc(mask_loaded, 16)
            sp.dma_start(sel_f[:], selector).then_inc(sel_loaded, 16)
            load_rest(0, 0)
            load_first(1, 1)
            load_rest(1, 1)
            with sp.Fori(0, TURNS - 1) as it:
                for par in range(TURN_HEADS):
                    for g in range(NCH):
                        store(it, par, g)
                    load_first(at(it, TURN_HEADS, TURN_HEADS + par), par)
                    load_rest(at(it, TURN_HEADS, TURN_HEADS + par), par)
            for par in range(TURN_HEADS):
                for g in range(NCH):
                    store(TURNS - 1, par, g)
                if par == 0:
                    heads.load_dilated(sp, qk_hi_d, qk_lo_d, toe_d, 0, 0)
            for par in range(2):
                sp.wait_ge(y_stored[par], 16 + 16 * TURNS * GROUPS // 2)

        @block.gpsimd
        def _(pool):
            pool.sem_inc(y_done, 2)
            pool.memset(zeros[:], 0.0).then_inc(pool_zeros_set, 1)
            pool.wait_ge(pool_zeros_set, 1)
            pool.memset(q_lo0[1][DH:P, :].bitcast(F32), 0.0).then_inc(pool_zeros_set, 1)
            pool.wait_ge(pool_zeros_set, 2)

            def differences(it, par):
                pool.wait_ge(v_loaded[par], at(it, 16 * V, 16 * V))
                n = at(it, 2 * 4, 4 * par)
                pool.tensor_tensor(v_diff[:], v_prev[par][:], v_cur[par][:], ALU.subtract).then_inc(dv_step, 1)
                pool.tensor_copy(v_end2[par][:, 0:DH], v_end[par][:]).then_inc(dv_step, 1)
                pool.wait_ge(dv_step, n + 2)
                pool.sem_inc(pool_passed, 1)
                pool.tensor_copy(dv[par][:, :, 0:DH], v_diff[:]).then_inc(dv_step, 1)
                pool.tensor_tensor(v_end2[par][:, DH:2 * DH], v_end[par][:],
                                   v_end2[par][:, 0:DH].bitcast(F32), ALU.subtract).then_inc(dv_step, 1)
                pool.wait_ge(dv_step, n + 4)
                pool.tensor_tensor(dv[par][:, :, DH:2 * DH], v_diff[:],
                                   dv[par][:, :, 0:DH].bitcast(F32), ALU.subtract).then_inc(dv_done, 1)
                pool.wait_ge(dv_done, at(it, 2, par + 1))

            def apply_gate(it, par, g):
                n = group_index(par, g)
                if g == 0:
                    pool.wait_ge(rest_loaded[par], at(it, 16 * REST, 16 * REST))
                pool.wait_ge(sum_done, 2 + at(it, GROUPS, n + 1))
                pool.wait_ge(y_stored[n % 2], at(it, 16 * GROUPS // 2, 16 * (n // 2 + 1)))
                pool.tensor_tensor(y_out[n % 2][:], y_sum[n % 2][:], gate[par][:, g * CH:(g + 1) * CH],
                                   ALU.mult).then_inc(y_done, 1)

            with pool.Fori(0, TURNS) as it:
                differences(it, 0)
                apply_gate(it, 0, 0)
                differences(it, 1)
                for g in range(1, NCH):
                    apply_gate(it, 0, g)
                for g in range(NCH):
                    apply_gate(it, 1, g)

        @block.tensor
        def _(pe):
            pe.sem_inc(t_done, W_SLOTS)
            pe.sem_inc(av_done, 4)
            pe.wait_ge(zeros_set, 1)
            pe.wait_ge(pool_zeros_set, 2)

            def scores(it, u, i):
                par, g, c = UNITS[u]
                n = turn_index(u) + i
                if (g, c, i) == (0, 0, 0):
                    pe.wait_ge(first_loaded[par], at(it, 16 * QK, 16 * QK))
                if (g, c, i) == (1, 1, 0):
                    pe.wait_ge(rest_loaded[par], at(it, 16 * REST, 16 * REST))
                pe.wait_ge(w_done, at(it, STEPS, n + 1))
                width = keys(i, g, c)
                q = slice(g * CH + i * P, g * CH + (i + 1) * P)
                k = slice(c * CH, c * CH + width)
                pe.matmul(z_ps[n % 2][:, 0:width], q_hi2[par][:, q], k_both[par][:, k],
                          start=True, stop=False)
                pe.matmul(z_ps[n % 2][:, 0:width], q_lo0[par][:, q], k_both[par][:, k],
                          start=False, stop=True).then_inc(z_done, 1)

            def transpose_block(it, u, j):
                par, g, c = UNITS[u]
                n = turn_index(u) + j
                if j == 0:
                    pe.wait_ge(scan_done, 4 + at(it, STEPS, n + QB))
                pe.wait_ge(lo_done, at(it, STEPS, n + 1))
                for i in range(first_block(j, g, c), QB):
                    last = pe.transpose(t_ps[n % 4][:, i * P:(i + 1) * P],
                                        W[(turn_index(u) + i) % W_SLOTS][:, j * P:(j + 1) * P], ident[:])
                last.then_inc(t_done, 1)

            def values(it, u, j):
                par, g, c = UNITS[u]
                n = turn_index(u) + j
                o = o_ps[g % 2]
                if (c, j) == (g, 0):
                    if g == 0:
                        pe.wait_ge(sel_done, 1)
                        pe.wait_ge(dv_done, at(it, 2, par + 1))
                    pe.wait_ge(sum_done, at(it, GROUPS, group_index(par, g) + 1))
                    pe.matmul(o[:], v_end2[par][:], sel[:, g * CH:(g + 1) * CH], start=True, stop=False)
                cols = slice(first_block(j, g, c) * P, CH)
                pe.wait_ge(lo_done, 4 + at(it, STEPS, n + 1))
                last = (c, j) == (0, QB - 1)
                pe.matmul(o[:, cols], dv[par][:, c * QB + j, :], WT_hi[n % 4][:, cols],
                          start=False, stop=False)
                pe.matmul(o[:, cols], dv[par][:, c * QB + j, :], WT_lo[n % 4][:, cols],
                          start=False, stop=last).then_inc(av_done, 1)

            with pe.Fori(0, TURNS) as it:
                for s in range(STEPS + VALUES_LAG):
                    if s < STEPS:
                        scores(it, s // QB, s % QB)
                    if 0 <= s - TRANSPOSE_LAG < STEPS:
                        transpose_block(it, (s - TRANSPOSE_LAG) // QB, (s - TRANSPOSE_LAG) % QB)
                    if s >= VALUES_LAG:
                        values(it, (s - VALUES_LAG) // QB, (s - VALUES_LAG) % QB)

        @block.scalar
        def _(act):
            act.sem_inc(w_done, 2)
            act.sem_inc(low_copied, 2)

            def survive(it, u, i):
                par, g, c = UNITS[u]
                n = turn_index(u) + i
                width = keys(i, g, c)
                act.wait_ge(z_done, at(it, STEPS, n + 1))
                act.wait_ge(scan_done, at(it, STEPS, n + 1))
                act.activation(w[n % 4][:, 0:width], z_ps[n % 2][:, 0:width], ACT.Sigmoid,
                               scale=-SCALE).then_inc(w_done, 1)

            def high_part(it, u, j):
                par, g, c = UNITS[u]
                n = turn_index(u) + j
                cols = slice(first_block(j, g, c) * P, CH)
                act.wait_ge(t_done, W_SLOTS + at(it, STEPS, n + 1))
                act.wait_ge(av_done, at(it, STEPS, n + 1))
                act.activation(WT_hi[n % 4][:, cols], t_ps[n % 4][:, cols], ACT.Copy).then_inc(hi_done, 1)

            def copy_low(it, u):
                par, g, c = UNITS[u]
                n = group_index(par, g)
                act.wait_ge(av_done, 4 + at(it, STEPS, turn_index(u) + QB))
                act.wait_ge(sum_done, at(it, GROUPS, n + 1))
                act.activation(o_low[n % 2][:], o_ps[g % 2][DH:P, :], ACT.Copy).then_inc(low_copied, 1)

            with act.Fori(0, TURNS) as it:
                for s in range(STEPS + VALUES_LAG + 2):
                    if 0 <= s - HIGH_LAG < STEPS:
                        high_part(it, (s - HIGH_LAG) // QB, (s - HIGH_LAG) % QB)
                    if s < STEPS:
                        survive(it, s // QB, s % QB)
                    u, i = divmod(s - VALUES_LAG - 1, QB)
                    if u >= 0 and i == QB - 1 and UNITS[u][2] == 0:
                        copy_low(it, u)

        @block.vector
        def _(dve):
            dve.sem_inc(scan_done, 4)
            dve.sem_inc(lo_done, 4)
            dve.sem_inc(sum_done, 2)

            def scan(it, u, i):
                par, g, c = UNITS[u]
                n = turn_index(u) + i
                width = keys(i, g, c)
                dve.wait_ge(w_done, 2 + at(it, STEPS, n + 1))
                dve.wait_ge(t_done, at(it, STEPS, turn_index(u) + QB))
                if c == g:
                    first = 1.0
                    above = ones_above[:, CH - width:CH]
                else:
                    dve.wait_ge(scan_done, 4 + at(it, STEPS, n - QB + 1))
                    first = W[(n - QB) % W_SLOTS][:, 0:1]
                    above = zeros[:, 0:width]
                dve.tensor_tensor_scan(W[n % W_SLOTS][:, 0:width][:, ::-1], w[n % 4][:, 0:width][:, ::-1],
                                       above[:, ::-1], first, ALU.mult, ALU.max).then_inc(scan_done, 1)

            def low_part(it, u, j):
                par, g, c = UNITS[u]
                n = turn_index(u) + j
                cols = slice(first_block(j, g, c) * P, CH)
                dve.wait_ge(hi_done, at(it, STEPS, n + 1))
                dve.wait_ge(av_done, at(it, STEPS, n + 1))
                dve.tensor_tensor(WT_lo[n % 4][:, cols], t_ps[n % 4][:, cols],
                                  WT_hi[n % 4][:, cols].bitcast(F32), ALU.subtract).then_inc(lo_done, 1)

            def add_halves(it, u):
                par, g, c = UNITS[u]
                n = group_index(par, g)
                dve.wait_ge(low_copied, 2 + at(it, GROUPS, n + 1))
                dve.wait_ge(y_done, at(it, GROUPS, n + 1))
                dve.tensor_tensor(y_sum[n % 2][:], o_ps[g % 2][0:DH, :], o_low[n % 2][:],
                                  ALU.add).then_inc(sum_done, 1)

            dve.memset(q_lo0[0][DH:P, :].bitcast(F32), 0.0).then_inc(zeros_set, 1)
            dve.wait_ge(sel_loaded, 16)
            dve.tensor_copy(sel[:], sel_f[:]).then_inc(sel_done, 1)
            dve.wait_ge(mask_loaded, 16)
            dve.wait_ge(pool_zeros_set, 1)
            with dve.Fori(0, TURNS) as it:
                for s in range(STEPS + VALUES_LAG + 2):
                    if s < STEPS:
                        scan(it, s // QB, s % QB)
                    if 0 <= s - LOW_LAG < STEPS:
                        low_part(it, (s - LOW_LAG) // QB, (s - LOW_LAG) % QB)
                    u, i = divmod(s - VALUES_LAG - 1, QB)
                    if u >= 0 and i == QB - 1 and UNITS[u][2] == 0:
                        add_halves(it, u)


def dilated_phase(nc, heads, qk_hi_d, qk_lo_d, gate_d, va_d, toe_d, ident, y_d):
    TURN_HEADS = 2
    PAIRS = HEADS // TURN_HEADS
    NTILE = TB
    ORDER = (2, 1, 0)

    def tiles_of(c):
        per = TB // DILATIONS[c]
        return [(r * per + n, r, n) for r in range(DILATIONS[c]) for n in range(per)]

    def make_bunches():
        out = []
        for c in ORDER:
            tiles, size = tiles_of(c), (4 if c == 2 else 2)
            for a in range(0, NTILE, size):
                col, bunch = 0, []
                for idx, r, n in tiles[a:a + size]:
                    nk = 1 if n == 0 else 2
                    bunch.append((c, idx, r, n, nk, col))
                    col += nk * P
                out.append((bunch, col))
        return out

    BUNCHES = make_bunches()
    NB = len(BUNCHES)
    STEPS = TURN_HEADS * NB
    OBANKS = 3 * NTILE // 4

    def bank_of(c, idx):
        return ORDER.index(c) * (NTILE // 4) + idx // 4

    LAG_T, LAG_H, LAG_L, LAG_V, LAG_O = 2, 2, 2, 3, 4
    WEIGH_AT, PAIR_AT = 2, 11
    SCORE_SLOTS, PART_SLOTS = 4, 4
    BANKS_AFTER = [[bank for bank in range(OBANKS)
                    if bank in [bank_of(t[0], t[1]) for t in bunch if t[1] % 4 == 3]] for bunch, _ in BUNCHES]
    with ExitStack() as stack:
        m = Memory(nc, stack)
        k_both, q_hi2, q_lo0, bias = heads.k_both, heads.q_hi2, heads.q_lo0, heads.bias
        v = [m.ring(f"va{c}_", 2, [P, TB, 2 * DH], F32R) for c in range(3)]
        neg_s = m.ring("neg_s", SCORE_SLOTS, [P, CH])
        prob = m.ring("prob", SCORE_SLOTS, [P, CH])
        PT_hi = m.ring("PT_hi", PART_SLOTS, [P, CH], F32R)
        PT_lo = m.ring("PT_lo", PART_SLOTS, [P, CH], F32R)
        o_low = m.ring("oa_low", 2, [P, 4, DH])
        rows = m.ring("rows", 2, [P, 3, NTILE, ROW])
        moved = m.sb("moved", [P, 2, NTILE, ROW])
        neg_m = m.sb("neg_m", [P, NTILE])
        diff = m.sb("diff", [P, 3, NTILE])
        weight = m.sb("weight", [P, 3, NTILE])
        den = m.sb("den", [P, 3, NTILE])
        factor = m.sb("factor", [P, 3, NTILE])
        y_pos = m.sb("y_pos", [P, TB, P])
        term = m.sb("term", [P, TB, DH])
        gate = m.sb("gate_a", [P, T])
        y_out = m.ring("ya_out", 2, [P, CH])
        s_ps, t_ps = m.banks("s_ps", 2), m.banks("pt_ps", 2)
        o_ps, y_ps = m.banks("oa_ps", 2), m.banks("y_ps", 2)
        move_d = [[nc.dram_tensor(f"move{c}{i}_d", [T, ROW], F32) for i in range(2)] for c in (1, 2)]
        qk_loaded, bias_loaded = heads.qk_loaded, heads.bias_loaded
        v_loaded = [m.sems(f"va{c}_loaded", 2) for c in range(3)]
        gate_loaded = m.sem("gate_a_loaded")
        s_done, min_done, exp_done = m.sem("s_done"), m.sem("min_done"), m.sem("exp_done")
        pt_done, hi_done, lo_done = m.sem("pt_done"), m.sem("pt_hi_done"), m.sem("pt_lo_done")
        pv_done, low_copied, rows_done = m.sem("pv_done"), m.sem("oa_low_copied"), m.sem("rows_done")
        rows_moved, rows_back = m.sem("rows_moved"), m.sem("rows_back")
        passed = m.sem("a_passed")
        small, diff_done, weigh_done = m.sem("small_step"), m.sem("diff_done"), m.sem("weigh_done")
        exp_small = m.sem("exp_small")
        pool_step, merged = m.sem("pool_step"), m.sem("merged")
        last_step, last_merged = m.sem("last_step"), m.sem("last_merged")
        y_done, gated = m.sem("y_transposed"), m.sem("gated")
        y_stored = m.sems("a_y_stored", 2)
        V_LOADS = (2, 4, 2)
        MOVES = 5
        SMALL = 6
        block = stack.enter_context(nc.Block())

        @block.sync
        def _(sp):
            def load_values(head, par):
                src = va_d[bass.ds(head, 1), :, :, :].rearrange("o t a d -> (o t) (a d)")
                for r in (0, 8):
                    sp.dma_start(v[2][par][:, r:r + 8, :].bitcast(F32),
                                 src.rearrange("(p r) x -> p r x", r=16)[:, r:r + 8, :]) \
                        .then_inc(v_loaded[2][par], 16)
                for r in range(4):
                    sp.dma_start(v[1][par][:, 4 * r:4 * r + 4, :].bitcast(F32),
                                 src.rearrange("(n p r) x -> r p n x", p=P, r=4)[r]) \
                        .then_inc(v_loaded[1][par], 16)
                for p in (0, DH):
                    sp.dma_start(v[0][par][p:p + DH].bitcast(F32),
                                 src.rearrange("(n p) x -> p n x", p=P)[p:p + DH]) \
                        .then_inc(v_loaded[0][par], 16)

            def finish(pair):
                for ch in range(NCH):
                    sp.wait_ge(gated, 2 + at(pair, NCH, ch + 1))
                    sp.dma_start(y_d[bass.ds(pair * P, P), ch * CH:(ch + 1) * CH],
                                 y_out[ch % 2][:]).then_inc(y_stored[ch % 2], 16)

            def load_gate(pair):
                sp.dma_start(gate[:], gate_d[bass.ds(pair * P, P), :]).then_inc(gate_loaded, 16)

            def move(it, par):
                h = at(it, 2, par)
                sp.wait_ge(rows_done, 2 + at(it, 2 * OBANKS, par * OBANKS + bank_of(2, NTILE - 1) + 1))
                sp.dma_start(move_d[1][par][:, :].rearrange("(p r) x -> p r x", r=DILATIONS[2]),
                             rows[par][:, 2, :, :]).then_inc(rows_moved, 16)
                sp.wait_ge(rows_done, 2 + at(it, 2 * OBANKS, par * OBANKS + bank_of(1, NTILE - 1) + 1))
                out = move_d[0][par][:, :].rearrange("(n p r) x -> r p n x", p=P, r=DILATIONS[1])
                for r in range(DILATIONS[1]):
                    sp.dma_start(out[r], rows[par][:, 1, 4 * r:4 * r + 4, :]).then_inc(rows_moved, 16)
                sp.wait_ge(merged, h + 1)
                sp.wait_ge(rows_moved, h * (16 * MOVES) + 16 * MOVES)
                for c in (1, 2):
                    sp.dma_start(moved[:, c - 1, :, :],
                                 move_d[c - 1][par][:, :].rearrange("(n p) x -> p n x", p=P)) \
                        .then_inc(rows_back, 16)

            sp.sem_inc(y_stored[0], 16)
            sp.sem_inc(y_stored[1], 16)
            load_values(0, 0)
            heads.load_dilated(sp, qk_hi_d, qk_lo_d, toe_d, 1, 1)
            load_values(1, 1)
            load_gate(0)
            with sp.Fori(0, PAIRS - 1) as it:
                for par in range(2):
                    move(it, par)
                    sp.wait_ge(rows_done, 2 + at(it, 2 * OBANKS, (par + 1) * OBANKS))
                    heads.load_dilated(sp, qk_hi_d, qk_lo_d, toe_d, at(it, 2, 2 + par), par)
                    load_values(at(it, 2, 2 + par), par)
                finish(it)
                load_gate(at(it, 1, 1))
            for par in range(2):
                move(PAIRS - 1, par)
            finish(PAIRS - 1)
            for i in range(2):
                sp.wait_ge(y_stored[i], 16 + 16 * PAIRS * NCH // 2)

        @block.tensor
        def _(pe):
            pe.sem_inc(pt_done, SCORE_SLOTS)
            pe.sem_inc(pv_done, PART_SLOTS)
            pe.sem_inc(y_done, NCH)

            def scores(it, b):
                par, bunch = b // NB, BUNCHES[b % NB][0]
                if b % NB == 0:
                    pe.wait_ge(qk_loaded[par], at(it, 16 * HeadTiles.QK_LOADS, 16 * HeadTiles.QK_LOADS))
                pe.wait_ge(min_done, at(it, STEPS, b + 1))
                for c, idx, r, n, nk, col in bunch:
                    d = DILATIONS[c]
                    q0 = r + d * P * n
                    k0 = r + d * P * (n - nk + 1)
                    q = slice(q0, q0 + d * (P - 1) + 1, d)
                    k = slice(k0, k0 + d * (nk * P - 1) + 1, d)
                    out = s_ps[b % 2][:, col:col + nk * P]
                    pe.matmul(out, q_hi2[par][:, q], k_both[par][:, k], start=True, stop=False)
                    last = pe.matmul(out, q_lo0[par][:, q], k_both[par][:, k], start=False, stop=True)
                last.then_inc(s_done, 1)

            def transpose_weights(it, b):
                width = BUNCHES[b % NB][1]
                pe.wait_ge(exp_done, SCORE_SLOTS + at(it, STEPS, b + 1))
                pe.wait_ge(lo_done, at(it, STEPS, b + 1))
                for col in range(0, width, P):
                    last = pe.transpose(t_ps[b % 2][:, col:col + P], prob[b % SCORE_SLOTS][:, col:col + P], ident[:])
                last.then_inc(pt_done, 1)

            def values(it, b):
                par, bunch = b // NB, BUNCHES[b % NB][0]
                pe.wait_ge(lo_done, 2 + at(it, STEPS, b + 1))
                for c, idx, r, n, nk, col in bunch:
                    bank = par * OBANKS + bank_of(c, idx)
                    if idx == 0:
                        pe.wait_ge(v_loaded[c][par], at(it, 16 * V_LOADS[c], 16 * V_LOADS[c]))
                    if idx % 4 == 0:
                        pe.wait_ge(rows_done, at(it, 2 * OBANKS, bank + 1))
                    out = o_ps[bank % 2][:, (idx % 4) * P:(idx % 4 + 1) * P]
                    for kb in range(nk):
                        w = slice(col + kb * P, col + (kb + 1) * P)
                        vk = v[c][par][:, idx - nk + 1 + kb, :]
                        pe.matmul(out, PT_hi[b % PART_SLOTS][:, w], vk, start=(kb == 0), stop=False)
                        last = pe.matmul(out, PT_lo[b % PART_SLOTS][:, w], vk, start=False, stop=(kb == nk - 1))
                last.then_inc(pv_done, 1)

            def transpose_pair(pair, last_pair=False):
                pe.wait_ge(merged, 1 + at(pair, 2, 1 if last_pair else 2))
                for ch in range(NCH):
                    if last_pair:
                        pe.wait_ge(last_merged, ch + 1)
                    pe.wait_ge(gated, at(pair, NCH, ch + 1))
                    for j in range(4):
                        last = pe.transpose(y_ps[ch % 2][:, j * P:(j + 1) * P],
                                            y_pos[:, ch * 4 + j, :], ident[:])
                    last.then_inc(y_done, 1)

            def turn(it, pair_before):
                for s in range(STEPS + LAG_V):
                    if s < STEPS:
                        scores(it, s)
                    if 0 <= s - LAG_T < STEPS:
                        transpose_weights(it, s - LAG_T)
                    if s >= LAG_V:
                        values(it, s - LAG_V)
                    if s == PAIR_AT and pair_before is not None:
                        transpose_pair(pair_before)

            turn(0, None)
            with pe.Fori(1, PAIRS) as it:
                turn(it, it - 1)
            transpose_pair(PAIRS - 1, last_pair=True)

        @block.scalar
        def _(act):
            act.sem_inc(exp_done, SCORE_SLOTS)
            act.sem_inc(low_copied, 2)

            def weights(it, b):
                par, bunch = b // NB, BUNCHES[b % NB][0]
                act.wait_ge(min_done, 2 + at(it, STEPS, b + 1))
                act.wait_ge(pt_done, at(it, STEPS, b + 1))
                for c, idx, r, n, nk, col in bunch:
                    last = act.activation(prob[b % SCORE_SLOTS][:, col:col + nk * P], neg_s[b % SCORE_SLOTS][:, col:col + nk * P],
                                          ACT.Exp, scale=-1.0, bias=rows[par][:, c, idx, DH:DH + 1],
                                          accum_out=rows[par][:, c, idx, DH + 1:DH + 2])
                last.then_inc(exp_done, 1)

            def high_part(it, b):
                width = BUNCHES[b % NB][1]
                act.wait_ge(pt_done, SCORE_SLOTS + at(it, STEPS, b + 1))
                act.wait_ge(pv_done, at(it, STEPS, b + 1))
                act.activation(PT_hi[b % PART_SLOTS][:, 0:width], t_ps[b % 2][:, 0:width], ACT.Copy).then_inc(hi_done, 1)

            def copy_low(it, par, bank, b):
                n = par * OBANKS + bank
                act.wait_ge(pv_done, PART_SLOTS + at(it, STEPS, b + 1))
                act.wait_ge(rows_done, at(it, 2 * OBANKS, n + 1))
                src = o_ps[n % 2][:].rearrange("p (i a d) -> p i a d", i=4, a=2)
                act.activation(o_low[n % 2][:], src[:, :, 1, :], ACT.Copy).then_inc(low_copied, 1)

            def exp_weights(it, par):
                act.wait_ge(diff_done, at(it, 2, par + 1))
                act.activation(weight[:], diff[:], ACT.Exp).then_inc(exp_small, 1)

            def turn(it, before):
                for s in range(STEPS + LAG_O + 1):
                    if 0 <= s - LAG_H < STEPS:
                        high_part(it, s - LAG_H)
                    if s < STEPS:
                        weights(it, s)
                    b = s - LAG_O
                    if 0 <= b < STEPS:
                        for bank in BANKS_AFTER[b % NB]:
                            copy_low(it, b // NB, bank, b)
                    if s == WEIGH_AT + NB:
                        exp_weights(it, 0)
                    if s == WEIGH_AT and before is not None:
                        exp_weights(before, 1)

            turn(0, None)
            with act.Fori(1, PAIRS) as it:
                turn(it, it - 1)
            exp_weights(PAIRS - 1, 1)

        @block.vector
        def _(dve):
            dve.sem_inc(min_done, 2)
            dve.sem_inc(lo_done, 2)
            dve.sem_inc(rows_done, 2)
            dve.sem_inc(gated, 2)

            def minima(it, b):
                par, bunch = b // NB, BUNCHES[b % NB][0]
                if b % NB == 0:
                    dve.wait_ge(bias_loaded[par], at(it, 48, 48))
                    if not (isinstance(it, int) and it == 0):
                        dve.wait_ge(merged, 1 + at(it, 2, par - 1))
                dve.wait_ge(s_done, at(it, STEPS, b + 1))
                dve.wait_ge(exp_done, at(it, STEPS, b + 1))
                dve.sem_inc(passed, 1)
                for c, idx, r, n, nk, col in bunch:
                    last = dve.tensor_tensor_reduce(
                        out=neg_s[b % SCORE_SLOTS][:, col:col + nk * P], in0=s_ps[b % 2][:, col:col + nk * P],
                        in1=bias[par][:, c, (2 - nk) * P:2 * P], scale=-SCALE, scalar=3e38,
                        op0=ALU.add, op1=ALU.min, accum_out=rows[par][:, c, idx, DH:DH + 1])
                last.then_inc(min_done, 1)

            def low_part(it, b):
                width = BUNCHES[b % NB][1]
                dve.wait_ge(hi_done, at(it, STEPS, b + 1))
                dve.wait_ge(pv_done, at(it, STEPS, b + 1))
                dve.tensor_tensor(PT_lo[b % PART_SLOTS][:, 0:width], t_ps[b % 2][:, 0:width],
                                  PT_hi[b % PART_SLOTS][:, 0:width].bitcast(F32), ALU.subtract).then_inc(lo_done, 1)

            def add_halves(it, par, bank, b):
                n = par * OBANKS + bank
                dve.wait_ge(low_copied, 2 + at(it, 2 * OBANKS, n + 1))
                src = o_ps[n % 2][:].rearrange("p (i a d) -> p i a d", i=4, a=2)
                c, quad = ORDER[bank // 4], bank % 4
                dve.tensor_tensor(rows[par][:, c, 4 * quad:4 * quad + 4, 0:DH], src[:, :, 0, :],
                                  o_low[n % 2][:], ALU.add).then_inc(rows_done, 1)

            def stat(par, c, k):
                t = rows[par][:, 0, :, :] if c == 0 else moved[:, c - 1, :, :]
                return t[:, :, DH + k]

            def step(ins, it, par, k):
                ins.then_inc(small, 1)
                dve.wait_ge(small, at(it, 2 * SMALL, par * SMALL + k))

            def weigh_maxima(it, par):
                dve.wait_ge(rows_back, at(it, 64, par * 32 + 32))
                step(dve.tensor_tensor(neg_m[:], stat(par, 0, 0), stat(par, 1, 0), ALU.min), it, par, 1)
                step(dve.tensor_tensor(neg_m[:], neg_m[:], stat(par, 2, 0), ALU.min), it, par, 2)
                for c in range(3):
                    last = dve.tensor_tensor(diff[:, c, :], neg_m[:], stat(par, c, 0), ALU.subtract)
                last.then_inc(diff_done, 1)

            def weigh_sums(it, par):
                dve.wait_ge(exp_small, at(it, 2, par + 1))
                for c in range(3):
                    last = dve.tensor_tensor(den[:, c, :], weight[:, c, :], stat(par, c, 1), ALU.mult)
                step(last, it, par, 3)
                step(dve.tensor_tensor(neg_m[:], den[:, 0, :], den[:, 1, :], ALU.add), it, par, 4)
                step(dve.tensor_tensor(neg_m[:], neg_m[:], den[:, 2, :], ALU.add), it, par, 5)
                step(dve.reciprocal(den[:, 0, :], neg_m[:]), it, par, 6)
                dve.wait_ge(merged, at(it, 2, par + 1))
                dve.tensor_tensor(factor[:], weight[:], den[:, 0, :].unsqueeze(1).broadcast_to([P, 3, NTILE]),
                                  ALU.mult).then_inc(weigh_done, 1)

            def apply_gate(pair, ch):
                if ch == 0:
                    dve.wait_ge(gate_loaded, at(pair, 16, 16))
                dve.wait_ge(y_done, NCH + at(pair, NCH, ch + 1))
                dve.wait_ge(y_stored[ch % 2], at(pair, 16 * NCH // 2, 16 * (ch // 2 + 1)))
                dve.tensor_tensor(y_out[ch % 2][:], y_ps[ch % 2][:], gate[:, ch * CH:(ch + 1) * CH],
                                  ALU.mult).then_inc(gated, 1)

            def merge_last(ch):
                tiles = slice(4 * ch, 4 * ch + 4)
                out, part = y_pos[:, tiles, DH:P], term[:, tiles, :]
                if ch == 0:
                    dve.wait_ge(merged, 2 * PAIRS)
                    dve.wait_ge(weigh_done, 2 * PAIRS)
                for c in range(3):
                    src = rows[1][:, 0, tiles, 0:DH] if c == 0 else moved[:, c - 1, tiles, 0:DH]
                    share = factor[:, c, tiles].unsqueeze(2).broadcast_to([P, 4, DH])
                    dve.tensor_tensor(out if c == 0 else part, src, share, ALU.mult).then_inc(last_step, 1)
                    if c > 0:
                        dve.wait_ge(last_step, 4 * ch + 2 * c)
                        last = dve.tensor_tensor(out, out, part, ALU.add)
                        if c == 1:
                            last.then_inc(last_step, 1)
                            dve.wait_ge(last_step, 4 * ch + 3)
                        else:
                            last.then_inc(last_merged, 1)

            def turn(it, before):
                for s in range(STEPS + LAG_O + 1):
                    if s < STEPS:
                        minima(it, s)
                    if 0 <= s - LAG_L < STEPS:
                        low_part(it, s - LAG_L)
                    b = s - LAG_O
                    if 0 <= b < STEPS:
                        for bank in BANKS_AFTER[b % NB]:
                            add_halves(it, b // NB, bank, b)
                    if s == WEIGH_AT + NB:
                        weigh_maxima(it, 0)
                    if s == WEIGH_AT and before is not None:
                        weigh_maxima(before, 1)
                    if s == WEIGH_AT + 1 + NB:
                        weigh_sums(it, 0)
                    if s == WEIGH_AT + 1 and before is not None:
                        weigh_sums(before, 1)
                    if s == PAIR_AT and before is not None:
                        for ch in range(NCH):
                            apply_gate(before, ch)

            turn(0, None)
            with dve.Fori(1, PAIRS) as it:
                turn(it, it - 1)
            weigh_maxima(PAIRS - 1, 1)
            weigh_sums(PAIRS - 1, 1)
            for ch in range(NCH):
                merge_last(ch)
                if ch > 0:
                    apply_gate(PAIRS - 1, ch - 1)
            apply_gate(PAIRS - 1, NCH - 1)

        @block.gpsimd
        def _(pool):
            def merge(it, par):
                h = at(it, 2, par)
                pool.wait_ge(weigh_done, h + 1)
                if par == 0:
                    pool.wait_ge(y_done, at(it, NCH, NCH))
                out = y_pos[:, :, par * DH:(par + 1) * DH]
                for c in range(3):
                    src = rows[par][:, 0, :, 0:DH] if c == 0 else moved[:, c - 1, :, 0:DH]
                    share = factor[:, c, :].unsqueeze(2).broadcast_to([P, TB, DH])
                    if c == 0:
                        pool.tensor_tensor(out, src, share, ALU.mult).then_inc(pool_step, 1)
                    else:
                        pool.tensor_tensor(term[:], src, share, ALU.mult).then_inc(pool_step, 1)
                        pool.wait_ge(pool_step, h * 4 + 2 * c)
                        last = pool.tensor_tensor(out, out, term[:], ALU.add)
                        if c == 1:
                            last.then_inc(pool_step, 1)
                            pool.wait_ge(pool_step, h * 4 + 3)
                        else:
                            last.then_inc(merged, 1)

            pool.sem_inc(merged, 1)
            with pool.Fori(0, PAIRS - 1) as it:
                merge(it, 0)
                merge(it, 1)
            merge(PAIRS - 1, 0)


def output_phase(nc, xhat_d, y_d, w_out, ln0_g, ln0_b, b_out, ln_g, ln_b, out):
    TURN_TILES = 2
    TURNS = TB // TURN_TILES
    HALVES = D // CH
    STEPS = TURN_TILES * HALVES
    with ExitStack() as stack:
        m = Memory(nc, stack)
        wo_raw = m.ring("wo_raw", 2, [P, D])
        wo_hi = m.sb("wo_hi", [P, KD, D], F32R)
        wo_lo = m.sb("wo_lo", [P, KD, D], F32R)
        y_sb = m.ring("y_sb", 2, [P, KD, P])
        y_hi = m.ring("y_hi", 2, [P, KD, P], F32R)
        y_lo = m.ring("y_lo", 2, [P, KD, P], F32R)
        xh = m.ring("xh4_", 2, [P, D])
        base = m.ring("base", 2, [P, D])
        u = m.ring("u", 2, [P, D])
        res = m.ring("res", 2, [P, D])
        g_res, b_res = m.sb("g_res", [P, D]), m.sb("b_res", [P, D])
        b_out_row = m.sb("b_out_row", [P, D])
        g_row, b_row = m.sb("g_row", [P, D]), m.sb("b_row", [P, D])
        stats = m.ring("stats4_", 2, [P, 12])
        mv = m.ring("mv4_", 2, [P, 2])
        rstd = m.ring("rstd4_", 2, [P, 1])
        neg_half = m.sb("neg_half4", [P, 1])
        acc = m.banks("out_ps", STEPS)
        wo_loaded, tile_loaded = m.sems("wo_loaded", 2), m.sems("tile_loaded", 2)
        rows_loaded, rows_ready = m.sem("rows_loaded"), m.sem("rows_ready")
        wo_hi_done, wo_split = m.sem("wo_hi_done"), m.sem("wo_split")
        y_hi_done, y_split = m.sem("y_hi_done"), m.sem("y_split")
        base_step, base_done = m.sem("base_step"), m.sem("base_done")
        mm_done, sum_done, stats_done, mv_done = (m.sem("out_mm_done"), m.sem("u_done"),
                                                  m.sem("stats4_done"), m.sem("mv4_done"))
        var_done, rstd_done, norm_step, res_done = (m.sem("var4_done"), m.sem("rstd4_done"),
                                                    m.sem("norm_step"), m.sem("res_done"))
        passed, pool_passed, sp_passed = m.sem("passed4_"), m.sem("pool_passed4_"), m.sem("sp_passed4_")
        stored = m.sems("out_stored", 2)
        block = stack.enter_context(nc.Block())

        @block.sync
        def _(sp):
            def load_tile(n, j):
                sp.dma_start(y_sb[j][:], y_d[:, bass.ds(n * P, P)].rearrange("(k p) t -> p k t", p=P)) \
                    .then_inc(tile_loaded[j], 16)
                sp.dma_start(xh[j][:], xhat_d[bass.ds(n * P, P), :]).then_inc(tile_loaded[j], 16)

            sp.sem_inc(stored[0], 16)
            sp.sem_inc(stored[1], 16)
            for k in range(KD):
                if k >= 2:
                    sp.wait_ge(wo_split, k - 1)
                sp.dma_start(wo_raw[k % 2][:], w_out[k * P:(k + 1) * P, :]).then_inc(wo_loaded[k % 2], 16)
                if k < 2:
                    load_tile(k, k)

            def store(it, j):
                n = at(it, TURN_TILES, j)
                sp.wait_ge(res_done, n + 1)
                sp.dma_start(out[bass.ds(n * P, P), :], res[j][:]).then_inc(stored[j], 16)

            with sp.Fori(0, TURNS - 1) as it:
                for j in range(TURN_TILES):
                    n = at(it, TURN_TILES, j)
                    sp.wait_ge(y_split, n + 1)
                    sp.sem_inc(sp_passed, 1)
                    sp.wait_ge(base_done, 2 + n + 1)
                    load_tile(n + TURN_TILES, j)
                    store(it, j)
            for j in range(TURN_TILES):
                store(TURNS - 1, j)
            for j in range(TURN_TILES):
                sp.wait_ge(stored[j], 16 + 16 * TURNS)

        @block.gpsimd
        def _(pool):
            pool.sem_inc(base_done, 2)
            pool.memset(neg_half[:], -0.5).then_inc(rows_ready, 1)
            pool.wait_ge(rows_loaded, 16 * 5)
            pool.tensor_scalar(g_res[:], g_res[:], ALPHA, None, ALU.mult).then_inc(rows_ready, 1)
            pool.tensor_scalar(b_res[:], b_res[:], ALPHA, None, ALU.mult).then_inc(rows_ready, 1)
            pool.wait_ge(rows_ready, 3)
            pool.tensor_tensor(b_res[:], b_res[:], b_out_row[:], ALU.add).then_inc(rows_ready, 1)
            pool.wait_ge(rows_ready, 4)

            def make_base(it, j):
                n = at(it, TURN_TILES, j)
                pool.wait_ge(tile_loaded[j], at(it, 32, 32))
                pool.wait_ge(sum_done, at(it, STEPS, 2 * (j + 1)))
                pool.tensor_tensor(base[j][:], xh[j][:], g_res[:], ALU.mult).then_inc(base_step, 1)
                pool.wait_ge(base_step, n + 1)
                pool.tensor_tensor(base[j][:], base[j][:], b_res[:], ALU.add).then_inc(base_done, 1)

            def make_rstd(it, j):
                n = at(it, TURN_TILES, j)
                pool.wait_ge(mv_done, n + 1)
                pool.sem_inc(pool_passed, 1)
                pool.tensor_scalar(rstd[j][:], mv[j][:, 1:2], EPS, None, ALU.add).then_inc(var_done, 1)
                pool.wait_ge(var_done, n + 1)
                pool.tensor_tensor(rstd[j][:], rstd[j][:], neg_half[:], ALU.pow).then_inc(rstd_done, 1)

            make_base(0, 0)
            with pool.Fori(0, TURNS - 1) as it:
                make_base(it, 1)
                make_rstd(it, 0)
                make_base(at(it, 1, 1), 0)
                make_rstd(it, 1)
            make_base(TURNS - 1, 1)
            make_rstd(TURNS - 1, 0)
            make_rstd(TURNS - 1, 1)

        @block.scalar
        def _(act):
            for row, src in ((g_res, ln0_g), (b_res, ln0_b), (b_out_row, b_out), (g_row, ln_g), (b_row, ln_b)):
                act.dma_start(row[:], src.partition_broadcast(P)).then_inc(rows_loaded, 16)

        @block.tensor
        def _(pe):
            def products(it, j, first):
                n = at(it, TURN_TILES, j)
                pe.wait_ge(y_split, n + 1)
                for half in range(HALVES):
                    s = j * HALVES + half
                    pe.wait_ge(sum_done, at(it, STEPS, s + 1))
                    cols = slice(half * CH, (half + 1) * CH)
                    for k in range(KD):
                        if first and half == 0:
                            pe.wait_ge(wo_split, k + 1)
                        for a, (y, w) in enumerate(((y_hi, wo_hi), (y_hi, wo_lo), (y_lo, wo_hi))):
                            last = pe.matmul(acc[s][:], y[j][:, k, :], w[:, k, cols],
                                             start=(k, a) == (0, 0), stop=(k, a) == (KD - 1, 2))
                    last.then_inc(mm_done, 1)

            for j in range(TURN_TILES):
                products(0, j, j == 0)
            with pe.Fori(1, TURNS) as it:
                for j in range(TURN_TILES):
                    products(it, j, False)

        @block.vector
        def _(dve):
            dve.sem_inc(sum_done, STEPS)

            def split_y(it, j):
                n = at(it, TURN_TILES, j)
                dve.wait_ge(tile_loaded[j], at(it, 32, 32))
                dve.tensor_copy(y_hi[j][:], y_sb[j][:]).then_inc(y_hi_done, 1)
                dve.wait_ge(y_hi_done, n + 1)
                dve.tensor_tensor(y_lo[j][:], y_sb[j][:], y_hi[j][:].bitcast(F32), ALU.subtract) \
                    .then_inc(y_split, 1)

            def add_base(it, j):
                n = at(it, TURN_TILES, j)
                dve.wait_ge(base_done, 2 + n + 1)
                for half in range(HALVES):
                    s = j * HALVES + half
                    cols = slice(half * CH, (half + 1) * CH)
                    dve.wait_ge(mm_done, at(it, STEPS, s + 1))
                    dve.tensor_tensor(u[j][:, cols], acc[s][:], base[j][:, cols], ALU.add) \
                        .then_inc(sum_done, 1)
                dve.wait_ge(sum_done, STEPS + at(it, STEPS, 2 * (j + 1)))
                for half in range(HALVES):
                    last = dve.bn_stats(stats[j][:, 6 * half:6 * half + 6], u[j][:, half * CH:(half + 1) * CH])
                last.then_inc(stats_done, 1)
                dve.wait_ge(stats_done, n + 1)
                dve.sem_inc(passed, 1)
                dve.bn_aggr(mv[j][:], stats[j][:]).then_inc(mv_done, 1)

            def normalise(it, j):
                n = at(it, TURN_TILES, j)
                dve.wait_ge(rstd_done, n + 1)
                dve.tensor_scalar(u[j][:], u[j][:], mv[j][:, 0:1], rstd[j][:], ALU.subtract, ALU.mult) \
                    .then_inc(norm_step, 1)
                dve.wait_ge(norm_step, at(it, 2 * TURN_TILES, 2 * j + 1))
                dve.wait_ge(stored[j], at(it, 16, 16))
                dve.tensor_tensor(res[j][:], u[j][:], g_row[:], ALU.mult).then_inc(norm_step, 1)
                dve.wait_ge(norm_step, at(it, 2 * TURN_TILES, 2 * j + 2))
                dve.tensor_tensor(res[j][:], res[j][:], b_row[:], ALU.add).then_inc(res_done, 1)

            def split_wo(k):
                dve.wait_ge(wo_loaded[k % 2], 16 * (k // 2 + 1))
                dve.tensor_copy(wo_hi[:, k, :], wo_raw[k % 2][:]).then_inc(wo_hi_done, 1)
                dve.wait_ge(wo_hi_done, k + 1)
                dve.tensor_tensor(wo_lo[:, k, :], wo_raw[k % 2][:], wo_hi[:, k, :].bitcast(F32),
                                  ALU.subtract).then_inc(wo_split, 1)

            split_wo(0)
            split_y(0, 0)
            for k in range(1, KD):
                split_wo(k)
            dve.wait_ge(rows_loaded, 16 * 5)
            split_y(0, 1)
            with dve.Fori(0, TURNS - 1) as it:
                for j in range(TURN_TILES):
                    add_base(it, j)
                    split_y(at(it, 1, 1), j)
                    normalise(it, j)
            for j in range(TURN_TILES):
                add_base(TURNS - 1, j)
                normalise(TURNS - 1, j)


def build(nc, x, ln0_g, ln0_b, w_tiles, w_out, b_out, ln_g, ln_b, rel_bias, onehot, selector, mask, out):
    xhat_d = nc.dram_tensor("xhat_d", [T, D], F32)
    toe_d = nc.dram_tensor("toe_d", [3, HEADS, P, TOE], F32)
    qk_hi_d = nc.dram_tensor("qk_hi_d", [4 * WIDTH, T], F32)
    qk_lo_d = nc.dram_tensor("qk_lo_d", [4 * WIDTH, T], F32)
    gate_d = nc.dram_tensor("gate_d", [2 * WIDTH, T], F32)
    va_d = nc.dram_tensor("va_d", [HEADS, T, 2, DH], F32)
    vb_d = nc.dram_tensor("vb_d", [T + 1, WIDTH], F32)
    y_d = nc.dram_tensor("y_d", [2 * WIDTH, T], F32)
    with ExitStack() as stack:
        ident = stack.enter_context(nc.sbuf_tensor("ident", [P, P], F32))
        with ExitStack() as front:
            h_hi = front.enter_context(nc.sbuf_tensor("h_hi", [P, KD, T], F32R))
            h_lo = front.enter_context(nc.sbuf_tensor("h_lo", [P, KD, T], F32R))
            norm_phase(nc, x, ln0_g, ln0_b, rel_bias, onehot, xhat_d, toe_d, ident, h_hi, h_lo)
            projection_phase(nc, w_tiles, qk_hi_d, qk_lo_d, gate_d, va_d, vb_d, ident, h_hi, h_lo)
        with ExitStack() as mixers:
            heads = HeadTiles(nc, mixers)
            stick_phase(nc, heads, qk_hi_d, qk_lo_d, gate_d, vb_d, toe_d, selector, mask, ident, y_d)
            dilated_phase(nc, heads, qk_hi_d, qk_lo_d, gate_d, va_d, toe_d, ident, y_d)
        output_phase(nc, xhat_d, y_d, w_out, ln0_g, ln0_b, b_out, ln_g, ln_b, out)


def lay_out(x, w_in):
    w = np.asarray(w_in)[0]
    cols = [w[:, c:c + tiles * P] for _, c, _, tiles in SEGMENTS]
    w = np.concatenate(cols, axis=1).reshape(KD, P, W_TILES, P)
    return np.ascontiguousarray(np.asarray(x)[0]), np.ascontiguousarray(w.transpose(2, 1, 0, 3))


def kernel(x, ln0_g, ln0_b, w_in, w_out, b_out, ln_g, ln_b, rel_bias):
    from concourse import bacc
    from concourse.bass_utils import run_bass_kernel_spmd

    x2, w_tiles = lay_out(x, w_in)
    arrays = {
        "in_x": x2, "in_ln0_g": np.asarray(ln0_g), "in_ln0_b": np.asarray(ln0_b),
        "in_w_tiles": w_tiles, "in_w_out": np.ascontiguousarray(np.asarray(w_out)[0]),
        "in_b_out": np.ascontiguousarray(np.asarray(b_out)[0]),
        "in_ln_g": np.ascontiguousarray(np.asarray(ln_g)[0]),
        "in_ln_b": np.ascontiguousarray(np.asarray(ln_b)[0]),
        "in_rel_bias": np.asarray(rel_bias),
        "in_onehot": bucket_onehot(), "in_selector": block_selector(), "in_mask": stick_mask(),
    }
    nc = bacc.Bacc("TRN2", target_bir_lowering=False, num_devices=1)
    args = [nc.dram_tensor(name, a.shape, mybir.dt.from_np(a.dtype), kind="ExternalInput").ap()
            for name, a in arrays.items()]
    out = nc.dram_tensor("out_dram", (T, D), F32, kind="ExternalOutput").ap()
    build(nc, *args, out)
    result = run_bass_kernel_spmd(nc, [arrays], core_ids=[0])
    return np.asarray(result.results[0]["out_dram"]).reshape(1, T, D)
```

```python
from contextlib import ExitStack

import numpy as np

import concourse.bass as bass
from concourse import mybir

F32 = mybir.dt.float32
F32R = mybir.dt.float32r
ALU = mybir.AluOpType
ACT = mybir.ActivationFunctionType

T = 2048
D = 1024
DH = 64
HEADS = 8
WIDTH = HEADS * DH
IN_COLS = 6 * WIDTH + 2 * WIDTH
GATE_COL = 6 * WIDTH
P = 128
KD = D // P
TB = T // P
CH = 512
NCH = T // CH
QB = CH // P
DILATIONS = (1, 4, 16)
BAND = 128
N_BUCKETS = 32
MAX_DISTANCE = 2048
TOE = 3 * P
MASKED = -1e30
EPS = 1e-5
ALPHA = 2.0 ** 0.25
SCALE = DH ** -0.5
ROW = DH + 2


def at(it, per_turn, n):
    return it * per_turn + n


def behind(it, before, s, steps, lag):
    if s >= lag:
        return (it, s - lag) if s - lag < steps else None
    return None if before is None else (before, s - lag + steps)


def bucket_onehot():
    oh = np.zeros((N_BUCKETS + 1, 3, TOE), np.float32)
    max_exact = N_BUCKETS // 2
    for c, dil in enumerate(DILATIONS):
        for u in range(TOE):
            delta = 2 * P - 1 - u
            if 0 <= delta <= BAND:
                dist = delta * dil
                if dist < max_exact:
                    b = dist
                else:
                    n = np.float32(dist)
                    b = max_exact + int(np.float32(np.log(n / np.float32(max_exact))
                                                   / np.log(MAX_DISTANCE / max_exact)
                                                   * (N_BUCKETS - max_exact)))
                    b = min(b, N_BUCKETS - 1)
                oh[b, c, u] = 1.0
            else:
                oh[N_BUCKETS, c, u] = 1.0
    return oh.reshape(N_BUCKETS + 1, 3 * TOE)


def block_selector():
    sel = np.zeros((TB, T), np.float32)
    for b in range(TB):
        sel[b, b * P:(b + 1) * P] = 1.0
    return sel


def stick_mask():
    m = np.zeros((P, CH), np.float32)
    for q in range(P):
        m[q, CH - P + q:] = 1.0
    return m


class Memory:

    def __init__(self, nc, stack):
        self.nc, self.stack = nc, stack

    def sb(self, name, shape, dtype=F32):
        return self.stack.enter_context(self.nc.sbuf_tensor(name, shape, dtype))

    def ps(self, name, shape=(P, CH)):
        return self.stack.enter_context(self.nc.psum_tensor(name, list(shape), F32))

    def ring(self, name, n, shape, dtype=F32):
        return [self.sb(f"{name}{i}", shape, dtype) for i in range(n)]

    def banks(self, name, n):
        return [self.ps(f"{name}{i}") for i in range(n)]

    def sems(self, name, n):
        return [self.sem(f"{name}{i}") for i in range(n)]

    def sem(self, name):
        return self.stack.enter_context(self.nc.semaphore(name))


def norm_phase(nc, x, ln_g, ln_b, rel_bias, onehot, toe, ident, mv, rstd, h_hi, h_lo):
    GROUPS = TB // QB
    STEPS = GROUPS * KD
    X_SLOTS, XH_SLOTS, FULL_SLOTS, T_SLOTS = 4, 8, 3, 4
    DVE_HIGH = [g * KD + k for g in (GROUPS - 1,) for k in (1, 3, 5, 7)]
    POOL_LOW = [g * KD + k for g in range(GROUPS - 1) for k in (6,)]
    ACT_HIGH = [step for step in range(STEPS) if step not in DVE_HIGH]
    DVE_LOW = [step for step in range(STEPS) if step not in POOL_LOW]

    def count(step, steps):
        return sum(s <= step for s in steps)

    with ExitStack() as stack:
        m = Memory(nc, stack)
        x_sb = m.ring("x_sb", X_SLOTS, [P, D])
        xh_sb = m.ring("xh_sb", XH_SLOTS, [P, D])
        h_full = m.ring("h_full", FULL_SLOTS, [P, CH])
        stats = m.ring("stats", 2, [P, 12])
        neg_half = m.sb("neg_half", [P, 1])
        g_col = m.sb("g_col", [P, KD])
        b_col = m.sb("b_col", [P, KD])
        rb = m.sb("rb", [N_BUCKETS + 1, HEADS])
        oh = m.sb("oh", [N_BUCKETS + 1, 3 * TOE])
        tp = m.banks("ln_tp", T_SLOTS)
        toe_ps = m.banks("toe_ps", 3)
        x_loaded = m.sems("x_loaded", X_SLOTS)
        col_loaded, rb_loaded = m.sem("col_loaded"), m.sem("rb_loaded")
        ident_step, rb_set, stats_done = m.sem("ident_step"), m.sem("rb_set"), m.sem("stats_done")
        mv_done, var_done, rstd_done = m.sem("mv_done"), m.sem("var_done"), m.sem("rstd_done")
        xh_done, tp_done = m.sem("xh_done"), m.sem("tp_done")
        full_done, act_high_done, dve_high_done = m.sem("full_done"), m.sem("act_high"), m.sem("dve_high")
        dve_low_done, pool_low_done = m.sem("dve_low"), m.sem("pool_low")
        toe_mm = m.sem("toe_mm")
        block = stack.enter_context(nc.Block())

        def wait_high(eng, step):
            if step in DVE_HIGH:
                eng.wait_ge(dve_high_done, count(step, DVE_HIGH))
            else:
                eng.wait_ge(act_high_done, count(step, ACT_HIGH))

        def low_part(eng, step, done):
            g, k = divmod(step, KD)
            wait_high(eng, step)
            cols = slice(g * CH, (g + 1) * CH)
            eng.tensor_tensor(h_lo[:, k, cols], h_full[step % FULL_SLOTS][:],
                              h_hi[:, k, cols].bitcast(F32), ALU.subtract).then_inc(done, 1)

        @block.sync
        def _(sp):
            for n in range(TB):
                if n >= X_SLOTS:
                    sp.wait_ge(xh_done, n - X_SLOTS + 1)
                sp.dma_start(x_sb[n % X_SLOTS][:], x[n * P:(n + 1) * P, :]) \
                    .then_inc(x_loaded[n % X_SLOTS], 16)
                if n == X_SLOTS - 1:
                    sp.wait_ge(rb_set, 2)
                    sp.dma_start(rb[0:N_BUCKETS, :], rel_bias).then_inc(rb_loaded, 16)
                    sp.dma_start(oh[:], onehot).then_inc(rb_loaded, 16)

        @block.gpsimd
        def _(pool):
            pool.memset(neg_half[:], -0.5).then_inc(rb_set, 1)
            pool.wait_ge(rb_set, 1)
            pool.memset(rb[:], MASKED).then_inc(rb_set, 1)
            pool.memset(ident[:], 0.0).then_inc(ident_step, 1)
            pool.wait_ge(ident_step, 1)
            pool.affine_select(out=ident[:], in_=ident[:], compare_op=ALU.not_equal, fill=1.0,
                               base=0, pattern=[[-1, P]], channel_multiplier=1) \
                .then_inc(ident_step, 1)
            pool.wait_ge(ident_step, 2)

            def deviation(n):
                pool.wait_ge(mv_done, n + 1)
                pool.tensor_scalar(rstd[:, n:n + 1], mv[:, n, 1:2], EPS, None, ALU.add) \
                    .then_inc(var_done, 1)
                pool.wait_ge(var_done, n + 1)
                pool.tensor_tensor(rstd[:, n:n + 1], rstd[:, n:n + 1], neg_half[:], ALU.pow) \
                    .then_inc(rstd_done, 1)

            for g in range(GROUPS + 1):
                before = [step for step in POOL_LOW if step // KD == g - 1]
                if g < GROUPS:
                    for n in range(g * QB, (g + 1) * QB):
                        deviation(n)
                        pool.wait_ge(rstd_done, n + 1)
                for step in before:
                    low_part(pool, step, pool_low_done)
                    pool.wait_ge(pool_low_done, count(step, POOL_LOW))

        @block.vector
        def _(dve):
            def moments(n):
                dve.wait_ge(x_loaded[n % X_SLOTS], 16 * (n // X_SLOTS + 1))
                for half in range(2):
                    last = dve.bn_stats(stats[n % 2][:, 6 * half:6 * half + 6],
                                        x_sb[n % X_SLOTS][:, half * CH:(half + 1) * CH])
                last.then_inc(stats_done, 1)
                dve.wait_ge(stats_done, n + 1)
                dve.bn_aggr(mv[:, n, :], stats[n % 2][:]).then_inc(mv_done, 1)

            def normalise(n):
                dve.wait_ge(rstd_done, n + 1)
                if n >= XH_SLOTS:
                    dve.wait_ge(tp_done, KD * ((n - XH_SLOTS) // QB + 1))
                dve.tensor_scalar(xh_sb[n % XH_SLOTS][:], x_sb[n % X_SLOTS][:], mv[:, n, 0:1],
                                  rstd[:, n:n + 1], ALU.subtract, ALU.mult).then_inc(xh_done, 1)

            def parts(step):
                g, k = divmod(step, KD)
                if step in DVE_HIGH:
                    dve.wait_ge(full_done, step + 1)
                    dve.tensor_copy(h_hi[:, k, g * CH:(g + 1) * CH], h_full[step % FULL_SLOTS][:]) \
                        .then_inc(dve_high_done, 1)
                if step not in POOL_LOW:
                    low_part(dve, step, dve_low_done)

            for g in range(GROUPS + 1):
                for k in range(KD):
                    if g < GROUPS and k < QB:
                        moments(g * QB + k)
                    if g > 0:
                        parts((g - 1) * KD + k)
                    if g < GROUPS and 0 < k <= QB:
                        normalise(g * QB + k - 1)

        @block.tensor
        def _(pe):
            pe.wait_ge(ident_step, 2)
            for g in range(GROUPS):
                pe.wait_ge(xh_done, QB * (g + 1))
                for k in range(KD):
                    step = g * KD + k
                    if step >= T_SLOTS:
                        before = step - T_SLOTS
                        pe.wait_ge(full_done, before + 1)
                        if before not in DVE_HIGH:
                            pe.wait_ge(act_high_done, count(before, ACT_HIGH))
                    for j in range(QB):
                        last = pe.transpose(tp[step % T_SLOTS][:, j * P:(j + 1) * P],
                                            xh_sb[(QB * g + j) % XH_SLOTS][:, k * P:(k + 1) * P], ident[:])
                    last.then_inc(tp_done, 1)
                if g == 0:
                    pe.wait_ge(rb_loaded, 32)
                    for c in range(3):
                        last = pe.matmul(toe_ps[c][0:HEADS, 0:TOE], rb[:], oh[:, c * TOE:(c + 1) * TOE],
                                         start=True, stop=True)
                    last.then_inc(toe_mm, 1)

        @block.scalar
        def _(act):
            with nc.allow_non_contiguous_dma("two short vectors"):
                act.dma_start(g_col[:], ln_g.rearrange("(k p) -> p k", p=P)).then_inc(col_loaded, 16)
                act.dma_start(b_col[:], ln_b.rearrange("(k p) -> p k", p=P)).then_inc(col_loaded, 16)
            act.wait_ge(col_loaded, 32)
            for step in range(STEPS):
                g, k = divmod(step, KD)
                act.wait_ge(tp_done, step + 1)
                if step >= FULL_SLOTS:
                    before = step - FULL_SLOTS
                    if before in POOL_LOW:
                        act.wait_ge(pool_low_done, count(before, POOL_LOW))
                    else:
                        act.wait_ge(dve_low_done, count(before, DVE_LOW))
                act.activation(h_full[step % FULL_SLOTS][:], tp[step % T_SLOTS][:], ACT.Identity,
                               scale=g_col[:, k:k + 1], bias=b_col[:, k:k + 1]).then_inc(full_done, 1)
                if step not in DVE_HIGH:
                    act.activation(h_hi[:, k, g * CH:(g + 1) * CH], tp[step % T_SLOTS][:], ACT.Identity,
                                   scale=g_col[:, k:k + 1], bias=b_col[:, k:k + 1]) \
                        .then_inc(act_high_done, 1)
                if step == 2 * KD:
                    act.wait_ge(toe_mm, 1)
                    for c in range(3):
                        act.activation(toe[:, c, :], toe_ps[c][0:HEADS, 0:TOE], ACT.Copy,
                                              scale=1.0 / SCALE)


SEGMENTS = (("qk", 0, 0, 8), ("qk", 3 * WIDTH, 2 * WIDTH, 8), ("gate", GATE_COL, 0, 8),
            ("va", 2 * WIDTH, 0, 4), ("vb", 5 * WIDTH, 0, 4))
W_TILES = sum(s[3] for s in SEGMENTS)


def segments():
    before = 0
    for kind, _, row, tiles in SEGMENTS:
        yield kind, row, tiles // 2, before
        before += tiles


def projection_phase(nc, w_tiles, toe, toe_d, qk_hi_d, qk_lo_d, gate_d, va_d, vb_d, ident, h_hi, h_lo):
    TILES = 2
    STEPS = TILES * NCH
    V_TILES = 24
    with ExitStack() as stack:
        m = Memory(nc, stack)
        w_raw = m.ring("w_raw", 2, [P, KD, P])
        w_hi = m.ring("w_hi", 2, [P, KD, P], F32R)
        w_lo = m.ring("w_lo", 2, [P, KD, P], F32R)
        st_hi = m.ring("st_hi", 2, [P, T], F32R)
        st_lo = m.ring("st_lo", 2, [P, T], F32R)
        vt = m.ring("vt", 2, [P, CH])
        zero_row = m.sb("zero_row", [1, DH])
        acc = m.banks("proj", 4)
        vtp = m.banks("vtp", 2)
        w_loaded = m.sems("w_loaded", 2)
        w_hi_done, w_split = m.sem("w_hi_done"), m.sem("w_split")
        proj_done, vt_done, vtp_done = m.sem("proj_done"), m.sem("vt_done"), m.sem("vtp_done")
        first_done, second_done = m.sem("first_done"), m.sem("second_done")
        hi_stored, lo_stored = m.sems("hi_stored", 2), m.sems("lo_stored", 2)
        zero_set, zero_stored = m.sem("zero_set"), m.sem("zero_stored")
        toe_stored = m.sem("toe_stored")
        block = stack.enter_context(nc.Block())

        @block.sync
        def _(sp):
            sp.wait_ge(zero_set, 1)
            sp.dma_start(vb_d[0:1, :].rearrange("o (h d) -> o h d", d=DH),
                         zero_row[:].unsqueeze(1).broadcast_to([1, HEADS, DH])).then_inc(zero_stored, 16)
            with sp.Fori(0, W_TILES // TILES) as it:
                for j in range(TILES):
                    sp.wait_ge(w_split, at(it, TILES, j + 1))
                    sp.dma_start(w_raw[j][:], w_tiles[bass.ds(at(it, TILES, j), 1)]
                                 .rearrange("o p k c -> (o p) k c")).then_inc(w_loaded[j], 16)
            sp.wait_ge(zero_stored, 16)

        @block.gpsimd
        def _(pool):
            pool.memset(zero_row[:], 0.0).then_inc(zero_set, 1)
            pool.wait_ge(w_split, 2 + TILES)
            for c in range(3):
                pool.dma_start(toe_d[c], toe[:, c, :].unsqueeze(1).broadcast_to([HEADS, P, TOE])) \
                    .then_inc(toe_stored, 16)
            pool.wait_ge(toe_stored, 16 * 3)

        @block.tensor
        def _(pe):
            pe.sem_inc(proj_done, 2 * NCH)
            pe.sem_inc(vtp_done, 2)

            def transpose_values(kind, base, it, s):
                step = base + at(it, STEPS, s)
                pe.wait_ge(vt_done, 4 + at(it, STEPS, s + 1) + (base - V_TILES * NCH))
                if kind == "va":
                    pe.wait_ge(second_done, 4 + step - 1)
                else:
                    pe.wait_ge(first_done, step - 1)
                for b in range(4):
                    last = pe.transpose(vtp[s % 2][:, b * P:(b + 1) * P],
                                        vt[s % 2][:, b * P:(b + 1) * P], ident[:])
                last.then_inc(vtp_done, 1)

            for kind, row, turns, before in segments():
                base = before * NCH
                if kind == "vb":
                    pe.wait_ge(second_done, 4 + base)
                if kind == "va":
                    pe.wait_ge(second_done, 4 + base)
                with pe.Fori(0, turns) as it:
                    for s in range(STEPS):
                        j, ch = divmod(s, NCH)
                        if ch == 0:
                            pe.wait_ge(w_split, 2 + before + at(it, TILES, j + 1))
                        if kind in ("qk", "gate"):
                            pe.wait_ge(second_done, base + at(it, STEPS, s + 1))
                        else:
                            pe.wait_ge(vt_done, base - V_TILES * NCH + at(it, STEPS, s + 1))
                        cols = slice(ch * CH, (ch + 1) * CH)
                        passes = [(w, h, k) for k in range(KD)
                                  for w, h in ((w_hi, h_hi), (w_hi, h_lo), (w_lo, h_hi))]
                        for n, (w, h, k) in enumerate(passes):
                            last = pe.matmul(acc[s % 4][:], w[j][:, k, :], h[:, k, cols],
                                             start=(n == 0), stop=(n == len(passes) - 1))
                        last.then_inc(proj_done, 1)
                        if kind in ("va", "vb") and s >= 1:
                            transpose_values(kind, base, it, s - 1)
                    if kind in ("va", "vb"):
                        transpose_values(kind, base, it, STEPS - 1)

        @block.scalar
        def _(act):
            for j in range(TILES):
                act.sem_inc(hi_stored[j], 32)
                act.sem_inc(lo_stored[j], 32)

            def store(kind, row, it, j, steps):
                act.wait_ge(first_done, steps)
                if kind != "vb":
                    act.wait_ge(second_done, 4 + steps)
                rows = bass.ds(at(it, TILES, j) * P + row, P)
                hi, lo = st_hi[j][:].bitcast(F32), st_lo[j][:].bitcast(F32)
                if kind == "qk":
                    act.sem_inc(hi_stored[j], 16)
                    act.sem_inc(lo_stored[j], 16)
                    act.dma_start(qk_hi_d[rows, :], hi).then_inc(hi_stored[j], 16)
                    act.dma_start(qk_lo_d[rows, :], lo).then_inc(lo_stored[j], 16)
                elif kind == "gate":
                    act.sem_inc(hi_stored[j], 32)
                    act.sem_inc(lo_stored[j], 16)
                    act.dma_start(gate_d[rows, :], lo).then_inc(lo_stored[j], 16)
                elif kind == "va":
                    for part, st, stored in ((0, hi, hi_stored[j]), (1, lo, lo_stored[j])):
                        src = st.rearrange("p (b h d) -> p b h d", b=TB, h=2)
                        for hh in range(2):
                            dst = va_d[bass.ds(at(it, 2 * TILES, 2 * j + hh), 1), :, part, :]
                            act.dma_start(dst.rearrange("o (b p) d -> p (o b) d", p=P),
                                          src[:, :, hh, :]).then_inc(stored, 16)
                else:
                    act.sem_inc(hi_stored[j], 16)
                    act.sem_inc(lo_stored[j], 32)
                    dst = vb_d[1:T + 1, bass.ds(at(it, TILES, j) * P, P)]
                    act.dma_start(dst.rearrange("(b p) c -> p b c", p=P),
                                  hi.rearrange("p (b c) -> p b c", b=TB)).then_inc(hi_stored[j], 16)

            for kind, row, turns, before in segments():
                base = before * NCH
                with act.Fori(0, turns) as it:
                    for s in range(STEPS):
                        j, ch = divmod(s, NCH)
                        cols = slice(ch * CH, (ch + 1) * CH)
                        if ch == 0:
                            act.wait_ge(hi_stored[j], 16 * before + at(it, 32, 32))
                        if kind in ("qk", "gate"):
                            act.wait_ge(proj_done, 2 * NCH + base + at(it, STEPS, s + 1))
                        else:
                            act.wait_ge(vtp_done, 2 + base - V_TILES * NCH + at(it, STEPS, s + 1))
                        if kind == "qk":
                            step = act.activation(st_hi[j][:, cols], acc[s % 4][:], ACT.Copy)
                        elif kind == "gate":
                            step = act.activation(st_hi[j][:, cols].bitcast(F32), acc[s % 4][:], ACT.Sigmoid)
                        elif kind == "va":
                            step = act.activation(st_hi[j][:, cols], vtp[s % 2][:], ACT.Copy)
                        else:
                            step = act.activation(st_hi[j][:, cols].bitcast(F32), vtp[s % 2][:], ACT.Copy)
                        step.then_inc(first_done, 1)
                        if s == NCH:
                            store(kind, row, it, 0, base + at(it, STEPS, NCH))
                    store(kind, row, it, 1, base + at(it, STEPS, STEPS))
            for j in range(TILES):
                act.wait_ge(hi_stored[j], 32 + 16 * W_TILES)
                act.wait_ge(lo_stored[j], 32 + 16 * W_TILES)

        @block.vector
        def _(dve):
            dve.sem_inc(w_split, 2)
            dve.sem_inc(second_done, 4)
            dve.sem_inc(vt_done, 4)

            def split_weights(slot, n):
                dve.wait_ge(w_loaded[slot], (n - slot) * 8 + 16)
                dve.wait_ge(proj_done, NCH * (n + 1))
                dve.tensor_copy(w_hi[slot][:], w_raw[slot][:]).then_inc(w_hi_done, 1)
                dve.wait_ge(w_hi_done, n + 1)
                dve.tensor_tensor(w_lo[slot][:], w_raw[slot][:], w_hi[slot][:].bitcast(F32),
                                  ALU.subtract).then_inc(w_split, 1)

            def low_part(base, it, s):
                j, ch = divmod(s, NCH)
                cols = slice(ch * CH, (ch + 1) * CH)
                dve.wait_ge(first_done, base + at(it, STEPS, s + 1))
                dve.tensor_tensor(st_lo[j][:, cols], vtp[s % 2][:], st_hi[j][:, cols].bitcast(F32),
                                  ALU.subtract).then_inc(second_done, 1)

            split_weights(0, 0)
            for kind, row, turns, before in segments():
                base = before * NCH
                def turn(it):
                    for s in range(STEPS):
                        j, ch = divmod(s, NCH)
                        cols = slice(ch * CH, (ch + 1) * CH)
                        step = base + at(it, STEPS, s + 1)
                        if ch == 0:
                            dve.wait_ge(lo_stored[j], 16 * before + at(it, 32, 32))
                        if kind == "qk":
                            dve.wait_ge(first_done, step)
                            dve.tensor_tensor(st_lo[j][:, cols], acc[s % 4][:],
                                              st_hi[j][:, cols].bitcast(F32),
                                              ALU.subtract).then_inc(second_done, 1)
                        elif kind == "gate":
                            dve.wait_ge(first_done, step)
                            dve.tensor_tensor(st_lo[j][:, cols].bitcast(F32), acc[s % 4][:],
                                              st_hi[j][:, cols].bitcast(F32),
                                              ALU.mult).then_inc(second_done, 1)
                        else:
                            dve.wait_ge(proj_done, 2 * NCH + step)
                            dve.wait_ge(vtp_done, step - V_TILES * NCH)
                            dve.tensor_copy(vt[s % 2][:], acc[s % 4][:]).then_inc(vt_done, 1)
                            if kind == "va" and s >= 1:
                                low_part(base, it, s - 1)
                        if ch == 0 and not (kind == "vb" and it == turns - 1 and j == TILES - 1):
                            split_weights(1 - j, before + at(it, TILES, j + 1))
                    if kind == "va":
                        low_part(base, it, STEPS - 1)

                if kind == "vb":
                    for it in range(turns):
                        turn(it)
                else:
                    with dve.Fori(0, turns) as it:
                        turn(it)


class HeadTiles:
    QK_LOADS = 5

    def __init__(self, nc, stack):
        m = Memory(nc, stack)
        self.k_both = m.ring("k_both", 2, [P, T], F32R)
        self.q_hi2 = m.ring("q_hi2", 2, [P, T], F32R)
        self.q_lo0 = m.ring("q_lo0", 2, [P, T], F32R)
        self.bias = m.ring("bias", 2, [P, 3, 2 * P])
        self.qk_loaded, self.bias_loaded = m.sems("a_qk_loaded", 2), m.sems("bias_loaded", 2)

    def qk_pieces(self, qk_hi_d, qk_lo_d, q, k, par, cols=slice(0, T)):
        parts = ((self.k_both, 0, qk_hi_d, k), (self.k_both, DH, qk_lo_d, k),
                 (self.q_hi2, 0, qk_hi_d, q), (self.q_hi2, DH, qk_hi_d, q), (self.q_lo0, 0, qk_lo_d, q))
        return [(tile[par][half:half + DH, cols].bitcast(F32), src[bass.ds(row, DH), cols])
                for tile, half, src, row in parts]

    def load_dilated(self, sp, qk_hi_d, qk_lo_d, toe_d, head, par):
        for dst, src in self.qk_pieces(qk_hi_d, qk_lo_d, head * DH, head * DH + WIDTH, par):
            sp.dma_start(dst, src).then_inc(self.qk_loaded[par], 16)
        for c in range(3):
            flat = toe_d[c, bass.ds(head, 1), :, :].rearrange("o a b -> o (a b)")
            band = flat[:, P - 1:P - 1 + P * (TOE - 1)].rearrange("o (i u) -> (o i) u", u=TOE - 1)
            sp.dma_start(self.bias[par][:, c, :], band[:, 0:2 * P]).then_inc(self.bias_loaded[par], 16)


def stick_phase(nc, heads, qk_hi_d, qk_lo_d, gate_d, vb_d, toe_d, selector, mask, ident, y_d):
    TURN_HEADS = 2
    TURNS = HEADS // TURN_HEADS
    UNITS = [(par, g, c) for par in range(TURN_HEADS) for g in range(NCH) for c in range(g, -1, -1)]
    STEPS = len(UNITS) * QB
    GROUPS = TURN_HEADS * NCH
    W_SLOTS = 16
    TRANSPOSE_LAG, HIGH_LAG, LOW_LAG, VALUES_LAG = 7, 8, 8, 11
    Q_ROW, K_ROW = 2 * WIDTH, 3 * WIDTH
    with ExitStack() as stack:
        m = Memory(nc, stack)
        k_both, q_hi2, q_lo0 = heads.k_both, heads.q_hi2, heads.q_lo0
        v_cur = m.ring("v_cur", 2, [P, TB, DH])
        v_prev = m.ring("v_prev", 2, [P, TB, DH])
        v_diff = m.sb("v_diff", [P, TB, DH])
        dv = m.ring("dv", 2, [P, TB, 2 * DH], F32R)
        v_end = m.ring("v_end", 2, [TB, DH])
        v_end2 = m.ring("v_end2", 2, [TB, 2 * DH], F32R)
        gate = m.ring("gate", 2, [DH, T])
        w = m.ring("w", 4, [P, CH])
        W = m.ring("W", W_SLOTS, [P, CH])
        WT_hi = m.ring("WT_hi", 4, [P, CH], F32R)
        WT_lo = m.ring("WT_lo", 4, [P, CH], F32R)
        o_low = m.ring("o_low", 2, [DH, CH])
        y_sum = m.ring("y_sum", 2, [DH, CH])
        y_out = m.ring("y_out", 2, [DH, CH])
        sel_f = m.sb("sel_f", [TB, T])
        sel = m.sb("sel", [TB, T], F32R)
        zeros = m.sb("zeros", [P, CH])
        ones_above = m.sb("ones_above", [P, CH])
        z_ps, t_ps, o_ps = m.banks("z_ps", 2), m.banks("wt_ps", 4), m.banks("o_ps", 2)
        first_loaded, second_loaded = m.sems("b_first_loaded", 2), m.sems("b_second_loaded", 2)
        v_loaded, rest_loaded = m.sems("b_v_loaded", 2), m.sems("b_rest_loaded", 2)
        y_stored = m.sems("b_y_stored", 2)
        sel_loaded, mask_loaded, sel_done = m.sem("sel_loaded"), m.sem("mask_loaded"), m.sem("sel_done")
        zeros_set, pool_zeros_set = m.sem("b_zeros_set"), m.sem("b_pool_zeros_set")
        pool_passed = m.sem("b_pool_passed")
        dv_step, dv_done = m.sem("dv_step"), m.sem("dv_done")
        z_done, w_done, scan_done = m.sem("z_done"), m.sem("w_done"), m.sem("scan_done")
        t_done, hi_done, lo_done = m.sem("wt_done"), m.sem("wt_hi_done"), m.sem("wt_lo_done")
        av_done, low_copied, sum_done, y_done = (m.sem("b_av_done"), m.sem("o_low_copied"),
                                                 m.sem("y_sum_done"), m.sem("b_y_done"))
        QK, V, REST = HeadTiles.QK_LOADS, 3, HeadTiles.QK_LOADS + 1
        block = stack.enter_context(nc.Block())

        def keys(i, g, c):
            return P * (i + 1) if c == g else CH

        def first_block(j, g, c):
            return j if c == g else 0

        def turn_index(u):
            return u * QB

        def group_index(par, g):
            return par * NCH + g

        def run_turns(eng, one_step):
            for s in range(STEPS):
                one_step(0, None, s)
            with eng.Fori(1, TURNS) as it:
                for s in range(STEPS):
                    one_step(it, it - 1, s)
            for s in range(STEPS, STEPS + VALUES_LAG + 1):
                one_step(TURNS - 1, None, s)

        @block.sync
        def _(sp):
            def load_first(head, par):
                for dst, src in heads.qk_pieces(qk_hi_d, qk_lo_d, head * DH + Q_ROW, head * DH + K_ROW,
                                                par, slice(0, CH)):
                    sp.dma_start(dst, src).then_inc(first_loaded[par], 16)

            def load_rest(head, par):
                for dst, src in ((v_cur[par][:], vb_d[1:T + 1, bass.ds(head * DH, DH)]
                                  .rearrange("(b p) d -> p b d", p=P)),
                                 (v_prev[par][:], vb_d[0:T, bass.ds(head * DH, DH)]
                                  .rearrange("(b p) d -> p b d", p=P)),
                                 (v_end[par][:], vb_d[P:T + 1:P, bass.ds(head * DH, DH)])):
                    sp.dma_start(dst, src).then_inc(v_loaded[par], 16)
                for dst, src in heads.qk_pieces(qk_hi_d, qk_lo_d, head * DH + Q_ROW, head * DH + K_ROW,
                                                par, slice(CH, 2 * CH)):
                    sp.dma_start(dst, src).then_inc(second_loaded[par], 16)
                pieces = heads.qk_pieces(qk_hi_d, qk_lo_d, head * DH + Q_ROW, head * DH + K_ROW, par,
                                         slice(2 * CH, T))
                pieces.append((gate[par][:], gate_d[bass.ds(head * DH + WIDTH, DH), :]))
                for dst, src in pieces:
                    sp.dma_start(dst, src).then_inc(rest_loaded[par], 16)

            def store(it, par, g):
                n = group_index(par, g)
                sp.wait_ge(y_done, 2 + at(it, GROUPS, n + 1))
                sp.dma_start(y_d[bass.ds(at(it, TURN_HEADS, par) * DH + WIDTH, DH), g * CH:(g + 1) * CH],
                             y_out[n % 2][:]).then_inc(y_stored[n % 2], 16)

            sp.sem_inc(y_stored[0], 16)
            sp.sem_inc(y_stored[1], 16)
            load_first(0, 0)
            sp.dma_start(sel_f[:], selector).then_inc(sel_loaded, 16)
            sp.dma_start(ones_above[:], mask).then_inc(mask_loaded, 16)
            load_rest(0, 0)
            load_first(1, 1)
            load_rest(1, 1)
            with sp.Fori(0, TURNS - 1) as it:
                for par in range(TURN_HEADS):
                    for g in range(NCH):
                        store(it, par, g)
                    load_first(at(it, TURN_HEADS, TURN_HEADS + par), par)
                    load_rest(at(it, TURN_HEADS, TURN_HEADS + par), par)
            for par in range(TURN_HEADS):
                for g in range(NCH):
                    store(TURNS - 1, par, g)
                if par == 0:
                    heads.load_dilated(sp, qk_hi_d, qk_lo_d, toe_d, 0, 0)
            for par in range(2):
                sp.wait_ge(y_stored[par], 16 + 16 * TURNS * GROUPS // 2)

        @block.gpsimd
        def _(pool):
            pool.sem_inc(y_done, 2)
            pool.memset(zeros[:], 0.0).then_inc(pool_zeros_set, 1)
            pool.wait_ge(pool_zeros_set, 1)
            pool.memset(q_lo0[1][DH:P, :].bitcast(F32), 0.0).then_inc(pool_zeros_set, 1)
            pool.wait_ge(pool_zeros_set, 2)

            pool.wait_ge(sel_loaded, 16)
            pool.tensor_copy(sel[:], sel_f[:]).then_inc(sel_done, 1)
            pool.wait_ge(sel_done, 1)

            def differences(it, par):
                pool.wait_ge(v_loaded[par], at(it, 16 * V, 16 * V))
                n = at(it, 2 * 4, 4 * par)
                pool.tensor_tensor(v_diff[:], v_prev[par][:], v_cur[par][:], ALU.subtract).then_inc(dv_step, 1)
                pool.tensor_copy(v_end2[par][:, 0:DH], v_end[par][:]).then_inc(dv_step, 1)
                pool.wait_ge(dv_step, n + 2)
                pool.sem_inc(pool_passed, 1)
                pool.tensor_copy(dv[par][:, :, 0:DH], v_diff[:]).then_inc(dv_step, 1)
                pool.tensor_tensor(v_end2[par][:, DH:2 * DH], v_end[par][:],
                                   v_end2[par][:, 0:DH].bitcast(F32), ALU.subtract).then_inc(dv_step, 1)
                pool.wait_ge(dv_step, n + 4)
                pool.tensor_tensor(dv[par][:, :, DH:2 * DH], v_diff[:],
                                   dv[par][:, :, 0:DH].bitcast(F32), ALU.subtract).then_inc(dv_done, 1)
                pool.wait_ge(dv_done, at(it, 2, par + 1))

            def apply_gate(it, par, g):
                n = group_index(par, g)
                if g == 0:
                    pool.wait_ge(rest_loaded[par], at(it, 16 * REST, 16 * REST))
                pool.wait_ge(sum_done, 2 + at(it, GROUPS, n + 1))
                pool.wait_ge(y_stored[n % 2], at(it, 16 * GROUPS // 2, 16 * (n // 2 + 1)))
                pool.tensor_tensor(y_out[n % 2][:], y_sum[n % 2][:], gate[par][:, g * CH:(g + 1) * CH],
                                   ALU.mult).then_inc(y_done, 1)

            def turn(it, last=False):
                apply_gate(it, 0, 0)
                differences(it, 1)
                for g in range(1, NCH):
                    apply_gate(it, 0, g)
                for g in range(NCH):
                    if g == 2 and not last:
                        differences(at(it, 1, 1), 0)
                    apply_gate(it, 1, g)

            differences(0, 0)
            with pool.Fori(0, TURNS - 1) as it:
                turn(it)
            turn(TURNS - 1, last=True)

        @block.tensor
        def _(pe):
            pe.sem_inc(t_done, W_SLOTS)
            pe.sem_inc(av_done, 4)
            pe.wait_ge(zeros_set, 1)
            pe.wait_ge(pool_zeros_set, 2)

            def scores(it, u, i):
                par, g, c = UNITS[u]
                n = turn_index(u) + i
                if (g, c, i) == (0, 0, 0):
                    pe.wait_ge(first_loaded[par], at(it, 16 * QK, 16 * QK))
                if (g, c, i) == (1, 1, 0):
                    pe.wait_ge(second_loaded[par], at(it, 16 * QK, 16 * QK))
                if (g, c, i) == (2, 2, 0):
                    pe.wait_ge(rest_loaded[par], at(it, 16 * REST, 16 * REST))
                pe.wait_ge(w_done, at(it, STEPS, n + 1))
                width = keys(i, g, c)
                q = slice(g * CH + i * P, g * CH + (i + 1) * P)
                k = slice(c * CH, c * CH + width)
                pe.matmul(z_ps[n % 2][:, 0:width], q_hi2[par][:, q], k_both[par][:, k],
                          start=True, stop=False)
                pe.matmul(z_ps[n % 2][:, 0:width], q_lo0[par][:, q], k_both[par][:, k],
                          start=False, stop=True).then_inc(z_done, 1)

            def transpose_block(it, u, j):
                par, g, c = UNITS[u]
                n = turn_index(u) + j
                if j == 0:
                    pe.wait_ge(scan_done, 4 + at(it, STEPS, n + QB))
                pe.wait_ge(lo_done, at(it, STEPS, n + 1))
                for i in range(first_block(j, g, c), QB):
                    last = pe.transpose(t_ps[n % 4][:, i * P:(i + 1) * P],
                                        W[(turn_index(u) + i) % W_SLOTS][:, j * P:(j + 1) * P], ident[:])
                last.then_inc(t_done, 1)

            def values(it, u, j):
                par, g, c = UNITS[u]
                n = turn_index(u) + j
                o = o_ps[g % 2]
                if (c, j) == (g, 0):
                    if g == 0:
                        pe.wait_ge(sel_done, 1)
                        pe.wait_ge(dv_done, at(it, 2, par + 1))
                    pe.wait_ge(sum_done, at(it, GROUPS, group_index(par, g) + 1))
                    pe.matmul(o[:], v_end2[par][:], sel[:, g * CH:(g + 1) * CH], start=True, stop=False)
                cols = slice(first_block(j, g, c) * P, CH)
                pe.wait_ge(lo_done, 4 + at(it, STEPS, n + 1))
                last = (c, j) == (0, QB - 1)
                pe.matmul(o[:, cols], dv[par][:, c * QB + j, :], WT_hi[n % 4][:, cols],
                          start=False, stop=False)
                pe.matmul(o[:, cols], dv[par][:, c * QB + j, :], WT_lo[n % 4][:, cols],
                          start=False, stop=last).then_inc(av_done, 1)

            def one_step(it, before, s):
                if s < STEPS:
                    scores(it, *divmod(s, QB))
                if then := behind(it, before, s, STEPS, TRANSPOSE_LAG):
                    transpose_block(then[0], *divmod(then[1], QB))
                if then := behind(it, before, s, STEPS, VALUES_LAG):
                    values(then[0], *divmod(then[1], QB))

            run_turns(pe, one_step)

        @block.scalar
        def _(act):
            act.sem_inc(w_done, 2)
            act.sem_inc(low_copied, 2)

            def survive(it, u, i):
                par, g, c = UNITS[u]
                n = turn_index(u) + i
                width = keys(i, g, c)
                act.wait_ge(z_done, at(it, STEPS, n + 1))
                act.wait_ge(scan_done, at(it, STEPS, n + 1))
                act.activation(w[n % 4][:, 0:width], z_ps[n % 2][:, 0:width], ACT.Sigmoid,
                               scale=-SCALE).then_inc(w_done, 1)

            def high_part(it, u, j):
                par, g, c = UNITS[u]
                n = turn_index(u) + j
                cols = slice(first_block(j, g, c) * P, CH)
                act.wait_ge(t_done, W_SLOTS + at(it, STEPS, n + 1))
                act.wait_ge(av_done, at(it, STEPS, n + 1))
                act.activation(WT_hi[n % 4][:, cols], t_ps[n % 4][:, cols], ACT.Copy).then_inc(hi_done, 1)

            def copy_low(it, u):
                par, g, c = UNITS[u]
                n = group_index(par, g)
                act.wait_ge(av_done, 4 + at(it, STEPS, turn_index(u) + QB))
                act.wait_ge(sum_done, at(it, GROUPS, n + 1))
                act.activation(o_low[n % 2][:], o_ps[g % 2][DH:P, :], ACT.Copy).then_inc(low_copied, 1)

            def one_step(it, before, s):
                if then := behind(it, before, s, STEPS, HIGH_LAG):
                    high_part(then[0], *divmod(then[1], QB))
                if s < STEPS:
                    survive(it, *divmod(s, QB))
                if then := behind(it, before, s, STEPS, VALUES_LAG + 1):
                    u, i = divmod(then[1], QB)
                    if i == QB - 1 and UNITS[u][2] == 0:
                        copy_low(then[0], u)

            run_turns(act, one_step)

        @block.vector
        def _(dve):
            dve.sem_inc(scan_done, 4)
            dve.sem_inc(lo_done, 4)
            dve.sem_inc(sum_done, 2)

            def scan(it, u, i):
                par, g, c = UNITS[u]
                n = turn_index(u) + i
                width = keys(i, g, c)
                dve.wait_ge(w_done, 2 + at(it, STEPS, n + 1))
                dve.wait_ge(t_done, at(it, STEPS, turn_index(u) + QB))
                if c == g:
                    first = 1.0
                    above = ones_above[:, CH - width:CH]
                else:
                    dve.wait_ge(scan_done, 4 + at(it, STEPS, n - QB + 1))
                    first = W[(n - QB) % W_SLOTS][:, 0:1]
                    above = zeros[:, 0:width]
                dve.tensor_tensor_scan(W[n % W_SLOTS][:, 0:width][:, ::-1], w[n % 4][:, 0:width][:, ::-1],
                                       above[:, ::-1], first, ALU.mult, ALU.max).then_inc(scan_done, 1)

            def low_part(it, u, j):
                par, g, c = UNITS[u]
                n = turn_index(u) + j
                cols = slice(first_block(j, g, c) * P, CH)
                dve.wait_ge(hi_done, at(it, STEPS, n + 1))
                dve.wait_ge(av_done, at(it, STEPS, n + 1))
                dve.tensor_tensor(WT_lo[n % 4][:, cols], t_ps[n % 4][:, cols],
                                  WT_hi[n % 4][:, cols].bitcast(F32), ALU.subtract).then_inc(lo_done, 1)

            def add_halves(it, u):
                par, g, c = UNITS[u]
                n = group_index(par, g)
                dve.wait_ge(low_copied, 2 + at(it, GROUPS, n + 1))
                dve.wait_ge(y_done, at(it, GROUPS, n + 1))
                dve.tensor_tensor(y_sum[n % 2][:], o_ps[g % 2][0:DH, :], o_low[n % 2][:],
                                  ALU.add).then_inc(sum_done, 1)

            dve.memset(q_lo0[0][DH:P, :].bitcast(F32), 0.0).then_inc(zeros_set, 1)
            dve.wait_ge(mask_loaded, 16)
            dve.wait_ge(pool_zeros_set, 1)
            def one_step(it, before, s):
                if s < STEPS:
                    scan(it, *divmod(s, QB))
                if then := behind(it, before, s, STEPS, LOW_LAG):
                    low_part(then[0], *divmod(then[1], QB))
                if then := behind(it, before, s, STEPS, VALUES_LAG + 1):
                    u, i = divmod(then[1], QB)
                    if i == QB - 1 and UNITS[u][2] == 0:
                        add_halves(then[0], u)

            run_turns(dve, one_step)


def dilated_phase(nc, heads, qk_hi_d, qk_lo_d, gate_d, va_d, toe_d, ident, y_d):
    TURN_HEADS = 2
    PAIRS = HEADS // TURN_HEADS
    NTILE = TB
    ORDER = (2, 1, 0)

    def tiles_of(c):
        per = TB // DILATIONS[c]
        return [(r * per + n, r, n) for r in range(DILATIONS[c]) for n in range(per)]

    def make_bunches():
        out = []
        for c in ORDER:
            tiles, size = tiles_of(c), (4 if c == 2 else 2)
            for a in range(0, NTILE, size):
                col, bunch = 0, []
                for idx, r, n in tiles[a:a + size]:
                    nk = 1 if n == 0 else 2
                    bunch.append((c, idx, r, n, nk, col))
                    col += nk * P
                out.append((bunch, col))
        return out

    BUNCHES = make_bunches()
    NB = len(BUNCHES)
    STEPS = TURN_HEADS * NB
    OBANKS = 3 * NTILE // 4

    def bank_of(c, idx):
        return ORDER.index(c) * (NTILE // 4) + idx // 4

    LAG_T, LAG_H, LAG_L, LAG_V, LAG_O = 2, 2, 2, 4, 5
    WEIGH_AT, PAIR_AT = 4, 13
    LAST_WEIGH = 4
    assert WEIGH_AT + 1 >= LAG_O
    SCORE_SLOTS, PART_SLOTS = 4, 4
    BANKS_AFTER = [[bank for bank in range(OBANKS)
                    if bank in [bank_of(t[0], t[1]) for t in bunch if t[1] % 4 == 3]] for bunch, _ in BUNCHES]
    with ExitStack() as stack:
        m = Memory(nc, stack)
        k_both, q_hi2, q_lo0, bias = heads.k_both, heads.q_hi2, heads.q_lo0, heads.bias
        v = [m.ring(f"va{c}_", 2, [P, TB, 2 * DH], F32R) for c in range(3)]
        neg_s = m.ring("neg_s", SCORE_SLOTS, [P, CH])
        prob = m.ring("prob", SCORE_SLOTS, [P, CH])
        PT_hi = m.ring("PT_hi", PART_SLOTS, [P, CH], F32R)
        PT_lo = m.ring("PT_lo", PART_SLOTS, [P, CH], F32R)
        o_low = m.ring("oa_low", 2, [P, 4, DH])
        rows = m.ring("rows", 2, [P, 3, NTILE, ROW])
        moved = m.sb("moved", [P, 2, NTILE, ROW])
        neg_m = m.sb("neg_m", [P, NTILE])
        diff = m.sb("diff", [P, 3, NTILE])
        weight = m.sb("weight", [P, 3, NTILE])
        den = m.sb("den", [P, 3, NTILE])
        factor = m.sb("factor", [P, 3, NTILE])
        y_pos = m.sb("y_pos", [P, TB, P])
        term = m.sb("term", [P, TB, DH])
        gate = m.sb("gate_a", [P, T])
        y_out = m.ring("ya_out", 2, [P, CH])
        s_ps, t_ps = m.banks("s_ps", 2), m.banks("pt_ps", 2)
        o_ps, y_ps = m.banks("oa_ps", 2), m.banks("y_ps", 2)
        move_d = [[nc.dram_tensor(f"move{c}{i}_d", [T, ROW], F32) for i in range(2)] for c in (1, 2)]
        qk_loaded, bias_loaded = heads.qk_loaded, heads.bias_loaded
        v_loaded = [m.sems(f"va{c}_loaded", 2) for c in range(3)]
        gate_loaded = m.sem("gate_a_loaded")
        s_done, min_done, exp_done = m.sem("s_done"), m.sem("min_done"), m.sem("exp_done")
        pt_done, hi_done, lo_done = m.sem("pt_done"), m.sem("pt_hi_done"), m.sem("pt_lo_done")
        pv_done, low_copied, rows_done = m.sem("pv_done"), m.sem("oa_low_copied"), m.sem("rows_done")
        second_moved, first_moved, rows_back = m.sem("second_moved"), m.sem("first_moved"), m.sem("rows_back")
        sp_passed = m.sem("a_sp_passed")
        passed = m.sem("a_passed")
        small, diff_done, weigh_done = m.sem("small_step"), m.sem("diff_done"), m.sem("weigh_done")
        exp_small = m.sem("exp_small")
        pool_step, merged = m.sem("pool_step"), m.sem("merged")
        last_step, last_merged = m.sem("last_step"), m.sem("last_merged")
        y_done, gated = m.sem("y_transposed"), m.sem("gated")
        y_stored = m.sems("a_y_stored", 2)
        V_LOADS = (2, 4, 2)
        SMALL = 6
        block = stack.enter_context(nc.Block())

        def run_turns(eng, one_step):
            for s in range(STEPS):
                one_step(0, None, s)
            with eng.Fori(1, PAIRS) as it:
                for s in range(STEPS):
                    one_step(it, it - 1, s)
            for s in range(STEPS, STEPS + max(LAG_O, LAST_WEIGH + 2)):
                one_step(PAIRS - 1, None, s)

        @block.sync
        def _(sp):
            def load_values(head, par):
                src = va_d[bass.ds(head, 1), :, :, :].rearrange("o t a d -> (o t) (a d)")
                for r in (0, 8):
                    sp.dma_start(v[2][par][:, r:r + 8, :].bitcast(F32),
                                 src.rearrange("(p r) x -> p r x", r=16)[:, r:r + 8, :]) \
                        .then_inc(v_loaded[2][par], 16)
                for r in range(4):
                    sp.dma_start(v[1][par][:, 4 * r:4 * r + 4, :].bitcast(F32),
                                 src.rearrange("(n p r) x -> r p n x", p=P, r=4)[r]) \
                        .then_inc(v_loaded[1][par], 16)
                for p in (0, DH):
                    sp.dma_start(v[0][par][p:p + DH].bitcast(F32),
                                 src.rearrange("(n p) x -> p n x", p=P)[p:p + DH]) \
                        .then_inc(v_loaded[0][par], 16)

            def finish(pair):
                for ch in range(NCH):
                    sp.wait_ge(gated, 2 + at(pair, NCH, ch + 1))
                    sp.dma_start(y_d[bass.ds(pair * P, P), ch * CH:(ch + 1) * CH],
                                 y_out[ch % 2][:]).then_inc(y_stored[ch % 2], 16)

            def load_gate(pair):
                sp.dma_start(gate[:], gate_d[bass.ds(pair * P, P), :]).then_inc(gate_loaded, 16)

            def move(it, par):
                h = at(it, 2, par)
                sp.wait_ge(rows_done, 2 + at(it, 2 * OBANKS, par * OBANKS + bank_of(2, NTILE - 1) + 1))
                sp.dma_start(move_d[1][par][:, :].rearrange("(p r) x -> p r x", r=DILATIONS[2]),
                             rows[par][:, 2, :, :]).then_inc(second_moved, 16)
                sp.wait_ge(merged, h + 1)
                sp.sem_inc(sp_passed, 1)
                sp.wait_ge(second_moved, h * 16 + 16)
                sp.dma_start(moved[:, 1, :, :], move_d[1][par][:, :].rearrange("(n p) x -> p n x", p=P)) \
                    .then_inc(rows_back, 16)
                sp.wait_ge(rows_done, 2 + at(it, 2 * OBANKS, par * OBANKS + bank_of(1, NTILE - 1) + 1))
                out = move_d[0][par][:, :].rearrange("(n p r) x -> r p n x", p=P, r=DILATIONS[1])
                for r in range(DILATIONS[1]):
                    sp.dma_start(out[r], rows[par][:, 1, 4 * r:4 * r + 4, :]).then_inc(first_moved, 16)
                sp.wait_ge(first_moved, h * (16 * DILATIONS[1]) + 16 * DILATIONS[1])
                sp.dma_start(moved[:, 0, :, :], move_d[0][par][:, :].rearrange("(n p) x -> p n x", p=P)) \
                    .then_inc(rows_back, 16)

            sp.sem_inc(y_stored[0], 16)
            sp.sem_inc(y_stored[1], 16)
            load_values(0, 0)
            heads.load_dilated(sp, qk_hi_d, qk_lo_d, toe_d, 1, 1)
            load_values(1, 1)
            load_gate(0)
            with sp.Fori(0, PAIRS - 1) as it:
                for par in range(2):
                    move(it, par)
                    sp.wait_ge(rows_done, 2 + at(it, 2 * OBANKS, (par + 1) * OBANKS))
                    heads.load_dilated(sp, qk_hi_d, qk_lo_d, toe_d, at(it, 2, 2 + par), par)
                    load_values(at(it, 2, 2 + par), par)
                finish(it)
                load_gate(at(it, 1, 1))
            for par in range(2):
                move(PAIRS - 1, par)
            finish(PAIRS - 1)
            for i in range(2):
                sp.wait_ge(y_stored[i], 16 + 16 * PAIRS * NCH // 2)

        @block.tensor
        def _(pe):
            pe.sem_inc(pt_done, SCORE_SLOTS)
            pe.sem_inc(pv_done, PART_SLOTS)
            pe.sem_inc(y_done, NCH)

            def scores(it, b):
                par, bunch = b // NB, BUNCHES[b % NB][0]
                if b % NB == 0:
                    pe.wait_ge(qk_loaded[par], at(it, 16 * HeadTiles.QK_LOADS, 16 * HeadTiles.QK_LOADS))
                pe.wait_ge(min_done, at(it, STEPS, b + 1))
                for c, idx, r, n, nk, col in bunch:
                    d = DILATIONS[c]
                    q0 = r + d * P * n
                    k0 = r + d * P * (n - nk + 1)
                    q = slice(q0, q0 + d * (P - 1) + 1, d)
                    k = slice(k0, k0 + d * (nk * P - 1) + 1, d)
                    out = s_ps[b % 2][:, col:col + nk * P]
                    pe.matmul(out, q_hi2[par][:, q], k_both[par][:, k], start=True, stop=False)
                    last = pe.matmul(out, q_lo0[par][:, q], k_both[par][:, k], start=False, stop=True)
                last.then_inc(s_done, 1)

            def transpose_weights(it, b):
                width = BUNCHES[b % NB][1]
                pe.wait_ge(exp_done, SCORE_SLOTS + at(it, STEPS, b + 1))
                pe.wait_ge(lo_done, at(it, STEPS, b + 1))
                for col in range(0, width, P):
                    last = pe.transpose(t_ps[b % 2][:, col:col + P], prob[b % SCORE_SLOTS][:, col:col + P], ident[:])
                last.then_inc(pt_done, 1)

            def values(it, b):
                par, bunch = b // NB, BUNCHES[b % NB][0]
                pe.wait_ge(lo_done, 2 + at(it, STEPS, b + 1))
                for c, idx, r, n, nk, col in bunch:
                    bank = par * OBANKS + bank_of(c, idx)
                    if idx == 0:
                        pe.wait_ge(v_loaded[c][par], at(it, 16 * V_LOADS[c], 16 * V_LOADS[c]))
                    if idx % 4 == 0:
                        pe.wait_ge(rows_done, at(it, 2 * OBANKS, bank + 1))
                    out = o_ps[bank % 2][:, (idx % 4) * P:(idx % 4 + 1) * P]
                    for kb in range(nk):
                        w = slice(col + kb * P, col + (kb + 1) * P)
                        vk = v[c][par][:, idx - nk + 1 + kb, :]
                        pe.matmul(out, PT_hi[b % PART_SLOTS][:, w], vk, start=(kb == 0), stop=False)
                        last = pe.matmul(out, PT_lo[b % PART_SLOTS][:, w], vk, start=False, stop=(kb == nk - 1))
                last.then_inc(pv_done, 1)

            def transpose_pair(pair, last_pair=False):
                pe.wait_ge(merged, 1 + at(pair, 2, 1 if last_pair else 2))
                for ch in range(NCH):
                    if last_pair:
                        pe.wait_ge(last_merged, ch + 1)
                    pe.wait_ge(gated, at(pair, NCH, ch + 1))
                    for j in range(4):
                        last = pe.transpose(y_ps[ch % 2][:, j * P:(j + 1) * P],
                                            y_pos[:, ch * 4 + j, :], ident[:])
                    last.then_inc(y_done, 1)

            def one_step(it, before, s):
                if s < STEPS:
                    scores(it, s)
                if then := behind(it, before, s, STEPS, LAG_T):
                    transpose_weights(*then)
                if then := behind(it, before, s, STEPS, LAG_V):
                    values(*then)
                if s == PAIR_AT and before is not None:
                    transpose_pair(before)

            run_turns(pe, one_step)
            transpose_pair(PAIRS - 1, last_pair=True)

        @block.scalar
        def _(act):
            act.sem_inc(exp_done, SCORE_SLOTS)
            act.sem_inc(low_copied, 2)

            def weights(it, b):
                par, bunch = b // NB, BUNCHES[b % NB][0]
                act.wait_ge(min_done, 2 + at(it, STEPS, b + 1))
                act.wait_ge(pt_done, at(it, STEPS, b + 1))
                for c, idx, r, n, nk, col in bunch:
                    last = act.activation(prob[b % SCORE_SLOTS][:, col:col + nk * P], neg_s[b % SCORE_SLOTS][:, col:col + nk * P],
                                          ACT.Exp, scale=-1.0, bias=rows[par][:, c, idx, DH:DH + 1],
                                          accum_out=rows[par][:, c, idx, DH + 1:DH + 2])
                last.then_inc(exp_done, 1)

            def high_part(it, b):
                width = BUNCHES[b % NB][1]
                act.wait_ge(pt_done, SCORE_SLOTS + at(it, STEPS, b + 1))
                act.wait_ge(pv_done, at(it, STEPS, b + 1))
                act.activation(PT_hi[b % PART_SLOTS][:, 0:width], t_ps[b % 2][:, 0:width], ACT.Copy).then_inc(hi_done, 1)

            def copy_low(it, par, bank, b):
                n = par * OBANKS + bank
                act.wait_ge(pv_done, PART_SLOTS + at(it, STEPS, b + 1))
                act.wait_ge(rows_done, at(it, 2 * OBANKS, n + 1))
                src = o_ps[n % 2][:].rearrange("p (i a d) -> p i a d", i=4, a=2)
                act.activation(o_low[n % 2][:], src[:, :, 1, :], ACT.Copy).then_inc(low_copied, 1)

            def exp_weights(it, par):
                act.wait_ge(diff_done, at(it, 2, par + 1))
                act.activation(weight[:], diff[:], ACT.Exp).then_inc(exp_small, 1)

            def one_step(it, before, s):
                if then := behind(it, before, s, STEPS, LAG_O):
                    turn, b = then
                    for bank in BANKS_AFTER[b % NB]:
                        copy_low(turn, b // NB, bank, b)
                if then := behind(it, before, s, STEPS, LAG_H):
                    high_part(*then)
                if s < STEPS:
                    weights(it, s)
                if s == WEIGH_AT + NB:
                    exp_weights(it, 0)
                if s == WEIGH_AT and before is not None:
                    exp_weights(before, 1)
                if s == STEPS + LAST_WEIGH:
                    exp_weights(it, 1)

            run_turns(act, one_step)

        @block.vector
        def _(dve):
            dve.sem_inc(min_done, 2)
            dve.sem_inc(lo_done, 2)
            dve.sem_inc(rows_done, 2)
            dve.sem_inc(gated, 2)

            def minima(it, b):
                par, bunch = b // NB, BUNCHES[b % NB][0]
                if b % NB == 0:
                    dve.wait_ge(bias_loaded[par], at(it, 48, 48))
                    if not (isinstance(it, int) and it == 0):
                        dve.wait_ge(merged, 1 + at(it, 2, par - 1))
                dve.wait_ge(s_done, at(it, STEPS, b + 1))
                dve.wait_ge(exp_done, at(it, STEPS, b + 1))
                dve.sem_inc(passed, 1)
                for c, idx, r, n, nk, col in bunch:
                    last = dve.tensor_tensor_reduce(
                        out=neg_s[b % SCORE_SLOTS][:, col:col + nk * P], in0=s_ps[b % 2][:, col:col + nk * P],
                        in1=bias[par][:, c, (2 - nk) * P:2 * P], scale=-SCALE, scalar=3e38,
                        op0=ALU.add, op1=ALU.min, accum_out=rows[par][:, c, idx, DH:DH + 1])
                last.then_inc(min_done, 1)

            def low_part(it, b):
                width = BUNCHES[b % NB][1]
                dve.wait_ge(hi_done, at(it, STEPS, b + 1))
                dve.wait_ge(pv_done, at(it, STEPS, b + 1))
                dve.tensor_tensor(PT_lo[b % PART_SLOTS][:, 0:width], t_ps[b % 2][:, 0:width],
                                  PT_hi[b % PART_SLOTS][:, 0:width].bitcast(F32), ALU.subtract).then_inc(lo_done, 1)

            def add_halves(it, par, bank, b):
                n = par * OBANKS + bank
                dve.wait_ge(low_copied, 2 + at(it, 2 * OBANKS, n + 1))
                src = o_ps[n % 2][:].rearrange("p (i a d) -> p i a d", i=4, a=2)
                c, quad = ORDER[bank // 4], bank % 4
                dve.tensor_tensor(rows[par][:, c, 4 * quad:4 * quad + 4, 0:DH], src[:, :, 0, :],
                                  o_low[n % 2][:], ALU.add).then_inc(rows_done, 1)

            def stat(par, c, k):
                t = rows[par][:, 0, :, :] if c == 0 else moved[:, c - 1, :, :]
                return t[:, :, DH + k]

            def step(ins, it, par, k):
                ins.then_inc(small, 1)
                dve.wait_ge(small, at(it, 2 * SMALL, par * SMALL + k))

            def weigh_maxima(it, par):
                dve.wait_ge(rows_back, at(it, 64, par * 32 + 32))
                step(dve.tensor_tensor(neg_m[:], stat(par, 0, 0), stat(par, 1, 0), ALU.min), it, par, 1)
                step(dve.tensor_tensor(neg_m[:], neg_m[:], stat(par, 2, 0), ALU.min), it, par, 2)
                for c in range(3):
                    last = dve.tensor_tensor(diff[:, c, :], neg_m[:], stat(par, c, 0), ALU.subtract)
                last.then_inc(diff_done, 1)

            def weigh_sums(it, par):
                dve.wait_ge(exp_small, at(it, 2, par + 1))
                for c in range(3):
                    last = dve.tensor_tensor(den[:, c, :], weight[:, c, :], stat(par, c, 1), ALU.mult)
                step(last, it, par, 3)
                step(dve.tensor_tensor(neg_m[:], den[:, 0, :], den[:, 1, :], ALU.add), it, par, 4)
                step(dve.tensor_tensor(neg_m[:], neg_m[:], den[:, 2, :], ALU.add), it, par, 5)
                step(dve.reciprocal(den[:, 0, :], neg_m[:]), it, par, 6)
                dve.wait_ge(merged, at(it, 2, par + 1))
                dve.tensor_tensor(factor[:], weight[:], den[:, 0, :].unsqueeze(1).broadcast_to([P, 3, NTILE]),
                                  ALU.mult).then_inc(weigh_done, 1)

            def apply_gate(pair, ch):
                if ch == 0:
                    dve.wait_ge(gate_loaded, at(pair, 16, 16))
                dve.wait_ge(y_done, NCH + at(pair, NCH, ch + 1))
                dve.wait_ge(y_stored[ch % 2], at(pair, 16 * NCH // 2, 16 * (ch // 2 + 1)))
                dve.tensor_tensor(y_out[ch % 2][:], y_ps[ch % 2][:], gate[:, ch * CH:(ch + 1) * CH],
                                  ALU.mult).then_inc(gated, 1)

            def merge_last(ch):
                tiles = slice(4 * ch, 4 * ch + 4)
                out, part = y_pos[:, tiles, DH:P], term[:, tiles, :]
                if ch == 0:
                    dve.wait_ge(merged, 2 * PAIRS)
                    dve.wait_ge(weigh_done, 2 * PAIRS)
                for c in range(3):
                    src = rows[1][:, 0, tiles, 0:DH] if c == 0 else moved[:, c - 1, tiles, 0:DH]
                    share = factor[:, c, tiles].unsqueeze(2).broadcast_to([P, 4, DH])
                    dve.tensor_tensor(out if c == 0 else part, src, share, ALU.mult).then_inc(last_step, 1)
                    if c > 0:
                        dve.wait_ge(last_step, 4 * ch + 2 * c)
                        last = dve.tensor_tensor(out, out, part, ALU.add)
                        if c == 1:
                            last.then_inc(last_step, 1)
                            dve.wait_ge(last_step, 4 * ch + 3)
                        else:
                            last.then_inc(last_merged, 1)

            def one_step(it, before, s):
                if s < STEPS:
                    minima(it, s)
                if then := behind(it, before, s, STEPS, LAG_O):
                    turn, b = then
                    for bank in BANKS_AFTER[b % NB]:
                        add_halves(turn, b // NB, bank, b)
                if then := behind(it, before, s, STEPS, LAG_L):
                    low_part(*then)
                for after, small_sums in ((0, weigh_maxima), (1, weigh_sums)):
                    if s == WEIGH_AT + after + NB:
                        small_sums(it, 0)
                    if s == WEIGH_AT + after and before is not None:
                        small_sums(before, 1)
                    if s == STEPS + LAST_WEIGH + after:
                        small_sums(it, 1)
                if s == PAIR_AT and before is not None:
                    for ch in range(NCH):
                        apply_gate(before, ch)

            run_turns(dve, one_step)
            for ch in range(NCH):
                merge_last(ch)
                if ch > 0:
                    apply_gate(PAIRS - 1, ch - 1)
            apply_gate(PAIRS - 1, NCH - 1)

        @block.gpsimd
        def _(pool):
            def merge(it, par):
                h = at(it, 2, par)
                pool.wait_ge(weigh_done, h + 1)
                if par == 0:
                    pool.wait_ge(y_done, at(it, NCH, NCH))
                out = y_pos[:, :, par * DH:(par + 1) * DH]
                for c in range(3):
                    src = rows[par][:, 0, :, 0:DH] if c == 0 else moved[:, c - 1, :, 0:DH]
                    share = factor[:, c, :].unsqueeze(2).broadcast_to([P, TB, DH])
                    if c == 0:
                        pool.tensor_tensor(out, src, share, ALU.mult).then_inc(pool_step, 1)
                    else:
                        pool.tensor_tensor(term[:], src, share, ALU.mult).then_inc(pool_step, 1)
                        pool.wait_ge(pool_step, h * 4 + 2 * c)
                        last = pool.tensor_tensor(out, out, term[:], ALU.add)
                        if c == 1:
                            last.then_inc(pool_step, 1)
                            pool.wait_ge(pool_step, h * 4 + 3)
                        else:
                            last.then_inc(merged, 1)

            pool.sem_inc(merged, 1)
            with pool.Fori(0, PAIRS - 1) as it:
                merge(it, 0)
                merge(it, 1)
            merge(PAIRS - 1, 0)


def output_phase(nc, x, mv_all, rstd_all, y_d, w_out, ln0_g, ln0_b, b_out, ln_g, ln_b, out):
    TURN_TILES = 2
    W_SLOTS = 8
    TURNS = TB // TURN_TILES
    HALVES = D // CH
    STEPS = TURN_TILES * HALVES
    with ExitStack() as stack:
        m = Memory(nc, stack)
        wo_raw = m.ring("wo_raw", W_SLOTS, [P, D])
        wo_hi = m.sb("wo_hi", [P, KD, D], F32R)
        wo_lo = m.sb("wo_lo", [P, KD, D], F32R)
        y_sb = m.ring("y_sb", 2, [P, KD, P])
        y_hi = m.ring("y_hi", 2, [P, KD, P], F32R)
        y_lo = m.ring("y_lo", 2, [P, KD, P], F32R)
        x_sb = m.ring("x4_", 2, [P, D])
        xh = m.ring("xh4_", 2, [P, D])
        base = m.ring("base", 2, [P, D])
        u = m.ring("u", 2, [P, D])
        res = m.ring("res", 2, [P, D])
        g_res, b_res = m.sb("g_res", [P, D]), m.sb("b_res", [P, D])
        b_out_row = m.sb("b_out_row", [P, D])
        g_row, b_row = m.sb("g_row", [P, D]), m.sb("b_row", [P, D])
        stats = m.ring("stats4_", 2, [P, 12])
        mv = m.ring("mv4_", 2, [P, 2])
        rstd = m.ring("rstd4_", 2, [P, 1])
        neg_half = m.sb("neg_half4", [P, 1])
        acc = m.banks("out_ps", STEPS)
        wo_loaded = m.sems("wo_loaded", W_SLOTS)
        y_loaded, x_loaded = m.sems("y4_loaded", 2), m.sems("x4_loaded", 2)
        res_rows_loaded, out_rows_loaded = m.sem("res_rows_loaded"), m.sem("out_rows_loaded")
        rows_scaled, rows_ready, neg_half_set = m.sem("rows_scaled"), m.sem("rows_ready"), m.sem("neg_half4_set")
        wo_hi_done, wo_split = m.sem("wo_hi_done"), m.sem("wo_split")
        y_hi_done, y_split = m.sem("y_hi_done"), m.sem("y_split")
        xh_ready = m.sem("xh4_ready")
        base_step, base_done = m.sem("base_step"), m.sem("base_done")
        mm_done, sum_done, stats_done, mv_done = (m.sem("out_mm_done"), m.sem("u_done"),
                                                  m.sem("stats4_done"), m.sem("mv4_done"))
        var_done, rstd_done, norm_step, res_done = (m.sem("var4_done"), m.sem("rstd4_done"),
                                                    m.sem("norm_step"), m.sem("res_done"))
        passed, pool_passed, sp_passed = m.sem("passed4_"), m.sem("pool_passed4_"), m.sem("sp_passed4_")
        stored = m.sems("out_stored", 2)
        block = stack.enter_context(nc.Block())

        @block.sync
        def _(sp):
            def load_y(n, j):
                sp.dma_start(y_sb[j][:], y_d[:, bass.ds(n * P, P)].rearrange("(k p) t -> p k t", p=P)) \
                    .then_inc(y_loaded[j], 16)

            def load_x(n, j):
                sp.dma_start(x_sb[j][:], x[bass.ds(n * P, P), :]).then_inc(x_loaded[j], 16)

            load_y(0, 0)

            for k in range(KD):
                if k >= W_SLOTS:
                    sp.wait_ge(wo_split, k - W_SLOTS + 1)
                sp.dma_start(wo_raw[k % W_SLOTS][:], w_out[k * P:(k + 1) * P, :]) \
                    .then_inc(wo_loaded[k % W_SLOTS], 16)
            load_y(1, 1)
            for row, src in ((g_res, ln0_g), (b_res, ln0_b), (b_out_row, b_out)):
                sp.dma_start(row[:], src.partition_broadcast(P)).then_inc(res_rows_loaded, 16)
            load_x(0, 0)
            load_x(1, 1)
            for row, src in ((g_row, ln_g), (b_row, ln_b)):
                sp.dma_start(row[:], src.partition_broadcast(P)).then_inc(out_rows_loaded, 16)

            with sp.Fori(0, TURNS - 1) as it:
                for j in range(TURN_TILES):
                    n = at(it, TURN_TILES, j)
                    sp.wait_ge(y_split, n + 1)
                    sp.sem_inc(sp_passed, 1)
                    sp.wait_ge(xh_ready, n + 1)
                    load_y(n + TURN_TILES, j)
                    load_x(n + TURN_TILES, j)

        @block.gpsimd
        def _(pool):
            pool.sem_inc(base_done, 2)
            pool.memset(neg_half[:], -0.5).then_inc(neg_half_set, 1)
            pool.wait_ge(neg_half_set, 1)
            pool.wait_ge(rows_ready, 1)

            def make_base(it, j):
                n = at(it, TURN_TILES, j)
                pool.wait_ge(xh_ready, n + 1)
                pool.wait_ge(sum_done, at(it, STEPS, 2 * (j + 1)))
                pool.tensor_tensor(base[j][:], xh[j][:], g_res[:], ALU.mult).then_inc(base_step, 1)
                pool.wait_ge(base_step, n + 1)
                pool.tensor_tensor(base[j][:], base[j][:], b_res[:], ALU.add).then_inc(base_done, 1)

            def make_rstd(it, j):
                n = at(it, TURN_TILES, j)
                pool.wait_ge(mv_done, n + 1)
                pool.sem_inc(pool_passed, 1)
                pool.tensor_scalar(rstd[j][:], mv[j][:, 1:2], EPS, None, ALU.add).then_inc(var_done, 1)
                pool.wait_ge(var_done, n + 1)
                pool.tensor_tensor(rstd[j][:], rstd[j][:], neg_half[:], ALU.pow).then_inc(rstd_done, 1)

            make_base(0, 0)
            with pool.Fori(0, TURNS - 1) as it:
                make_base(it, 1)
                make_rstd(it, 0)
                make_base(at(it, 1, 1), 0)
                make_rstd(it, 1)
            make_base(TURNS - 1, 1)
            make_rstd(TURNS - 1, 0)
            make_rstd(TURNS - 1, 1)

        @block.scalar
        def _(act):
            def high_wo(k):
                act.wait_ge(wo_loaded[k % W_SLOTS], 16 * (k // W_SLOTS + 1))
                act.activation(wo_hi[:, k, :], wo_raw[k % W_SLOTS][:], ACT.Copy).then_inc(wo_hi_done, 1)

            def high_y(it, j):
                n = at(it, TURN_TILES, j)
                act.wait_ge(y_loaded[j], at(it, 16, 16))
                act.wait_ge(sum_done, at(it, STEPS, 2 * (j + 1)))
                act.activation(y_hi[j][:], y_sb[j][:], ACT.Copy).then_inc(y_hi_done, 1)

            act.sem_inc(stored[0], 16)
            act.sem_inc(stored[1], 16)
            high_y(0, 0)
            for k in range(KD):
                high_wo(k)
            high_y(0, 1)
            act.wait_ge(res_rows_loaded, 16 * 3)
            for row in (g_res, b_res):
                act.activation(row[:], row[:], ACT.Copy, scale=ALPHA).then_inc(rows_scaled, 1)

            def store(it, j):
                n = at(it, TURN_TILES, j)
                act.wait_ge(res_done, n + 1)
                act.dma_start(out[bass.ds(n * P, P), :], res[j][:]).then_inc(stored[j], 16)

            with act.Fori(0, TURNS - 1) as it:
                for j in range(TURN_TILES):
                    high_y(at(it, 1, 1), j)
                    store(it, j)
            for j in range(TURN_TILES):
                store(TURNS - 1, j)
            for j in range(TURN_TILES):
                act.wait_ge(stored[j], 16 + 16 * TURNS)

        @block.tensor
        def _(pe):
            def products(it, j, first):
                n = at(it, TURN_TILES, j)
                pe.wait_ge(y_split, n + 1)
                for half in range(HALVES):
                    s = j * HALVES + half
                    pe.wait_ge(sum_done, at(it, STEPS, s + 1))
                    cols = slice(half * CH, (half + 1) * CH)
                    for k in range(KD):
                        if first and half == 0:
                            pe.wait_ge(wo_split, k + 1)
                        for a, (y, w) in enumerate(((y_hi, wo_hi), (y_hi, wo_lo), (y_lo, wo_hi))):
                            last = pe.matmul(acc[s][:], y[j][:, k, :], w[:, k, cols],
                                             start=(k, a) == (0, 0), stop=(k, a) == (KD - 1, 2))
                    last.then_inc(mm_done, 1)

            for j in range(TURN_TILES):
                products(0, j, j == 0)
            with pe.Fori(1, TURNS) as it:
                for j in range(TURN_TILES):
                    products(it, j, False)

        @block.vector
        def _(dve):
            dve.sem_inc(sum_done, STEPS)

            def split_y(it, j):
                n = at(it, TURN_TILES, j)
                dve.wait_ge(y_hi_done, n + 1)
                dve.tensor_tensor(y_lo[j][:], y_sb[j][:], y_hi[j][:].bitcast(F32), ALU.subtract) \
                    .then_inc(y_split, 1)

            def normalise_x(it, j):
                n = at(it, TURN_TILES, j)
                dve.wait_ge(x_loaded[j], at(it, 16, 16))
                dve.wait_ge(base_done, n + 1)
                dve.tensor_scalar(xh[j][:], x_sb[j][:], mv_all[:, bass.ds(n, 1), 0:1].rearrange("p o a -> p (o a)"),
                                  rstd_all[:, bass.ds(n, 1)], ALU.subtract, ALU.mult).then_inc(xh_ready, 1)

            def add_base(it, j):
                n = at(it, TURN_TILES, j)
                dve.wait_ge(base_done, 2 + n + 1)
                for half in range(HALVES):
                    s = j * HALVES + half
                    cols = slice(half * CH, (half + 1) * CH)
                    dve.wait_ge(mm_done, at(it, STEPS, s + 1))
                    dve.tensor_tensor(u[j][:, cols], acc[s][:], base[j][:, cols], ALU.add) \
                        .then_inc(sum_done, 1)
                dve.wait_ge(sum_done, STEPS + at(it, STEPS, 2 * (j + 1)))
                for half in range(HALVES):
                    last = dve.bn_stats(stats[j][:, 6 * half:6 * half + 6], u[j][:, half * CH:(half + 1) * CH])
                last.then_inc(stats_done, 1)
                dve.wait_ge(stats_done, n + 1)
                dve.sem_inc(passed, 1)
                dve.bn_aggr(mv[j][:], stats[j][:]).then_inc(mv_done, 1)

            def normalise(it, j):
                n = at(it, TURN_TILES, j)
                dve.wait_ge(rstd_done, n + 1)
                dve.wait_ge(out_rows_loaded, 16 * 2)
                dve.tensor_scalar(u[j][:], u[j][:], mv[j][:, 0:1], rstd[j][:], ALU.subtract, ALU.mult) \
                    .then_inc(norm_step, 1)
                dve.wait_ge(norm_step, at(it, 2 * TURN_TILES, 2 * j + 1))
                dve.wait_ge(stored[j], at(it, 16, 16))
                dve.tensor_tensor(res[j][:], u[j][:], g_row[:], ALU.mult).then_inc(norm_step, 1)
                dve.wait_ge(norm_step, at(it, 2 * TURN_TILES, 2 * j + 2))
                dve.tensor_tensor(res[j][:], res[j][:], b_row[:], ALU.add).then_inc(res_done, 1)

            def split_wo(k):
                dve.wait_ge(wo_hi_done, k + 1)
                dve.tensor_tensor(wo_lo[:, k, :], wo_raw[k % W_SLOTS][:], wo_hi[:, k, :].bitcast(F32),
                                  ALU.subtract).then_inc(wo_split, 1)

            split_y(0, 0)
            for k in range(KD):
                split_wo(k)
            split_y(0, 1)
            normalise_x(0, 0)
            dve.wait_ge(rows_scaled, 2)
            dve.tensor_tensor(b_res[:], b_res[:], b_out_row[:], ALU.add).then_inc(rows_ready, 1)
            normalise_x(0, 1)
            with dve.Fori(0, TURNS - 1) as it:
                for j in range(TURN_TILES):
                    add_base(it, j)
                    normalise_x(at(it, 1, 1), j)
                    split_y(at(it, 1, 1), j)
                    normalise(it, j)
            for j in range(TURN_TILES):
                add_base(TURNS - 1, j)
                normalise(TURNS - 1, j)


def build(nc, x, ln0_g, ln0_b, w_tiles, w_out, b_out, ln_g, ln_b, rel_bias, onehot, selector, mask, out):
    toe_d = nc.dram_tensor("toe_d", [3, HEADS, P, TOE], F32)
    qk_hi_d = nc.dram_tensor("qk_hi_d", [4 * WIDTH, T], F32)
    qk_lo_d = nc.dram_tensor("qk_lo_d", [4 * WIDTH, T], F32)
    gate_d = nc.dram_tensor("gate_d", [2 * WIDTH, T], F32)
    va_d = nc.dram_tensor("va_d", [HEADS, T, 2, DH], F32)
    vb_d = nc.dram_tensor("vb_d", [T + 1, WIDTH], F32)
    y_d = nc.dram_tensor("y_d", [2 * WIDTH, T], F32)
    with ExitStack() as stack:
        ident = stack.enter_context(nc.sbuf_tensor("ident", [P, P], F32))
        mv = stack.enter_context(nc.sbuf_tensor("mv", [P, TB, 2], F32))
        rstd = stack.enter_context(nc.sbuf_tensor("rstd", [P, TB], F32))
        with ExitStack() as front:
            toe = front.enter_context(nc.sbuf_tensor("toe", [HEADS, 3, TOE], F32))
            h_hi = front.enter_context(nc.sbuf_tensor("h_hi", [P, KD, T], F32R))
            h_lo = front.enter_context(nc.sbuf_tensor("h_lo", [P, KD, T], F32R))
            norm_phase(nc, x, ln0_g, ln0_b, rel_bias, onehot, toe, ident, mv, rstd, h_hi, h_lo)
            projection_phase(nc, w_tiles, toe, toe_d, qk_hi_d, qk_lo_d, gate_d, va_d, vb_d, ident, h_hi, h_lo)
        with ExitStack() as mixers:
            heads = HeadTiles(nc, mixers)
            stick_phase(nc, heads, qk_hi_d, qk_lo_d, gate_d, vb_d, toe_d, selector, mask, ident, y_d)
            dilated_phase(nc, heads, qk_hi_d, qk_lo_d, gate_d, va_d, toe_d, ident, y_d)
        output_phase(nc, x, mv, rstd, y_d, w_out, ln0_g, ln0_b, b_out, ln_g, ln_b, out)


def lay_out(x, w_in):
    w = np.asarray(w_in)[0]
    cols = [w[:, c:c + tiles * P] for _, c, _, tiles in SEGMENTS]
    w = np.concatenate(cols, axis=1).reshape(KD, P, W_TILES, P)
    return np.ascontiguousarray(np.asarray(x)[0]), np.ascontiguousarray(w.transpose(2, 1, 0, 3))


def kernel(x, ln0_g, ln0_b, w_in, w_out, b_out, ln_g, ln_b, rel_bias):
    from concourse import bacc
    from concourse.bass_utils import run_bass_kernel_spmd

    x2, w_tiles = lay_out(x, w_in)
    arrays = {
        "in_x": x2, "in_ln0_g": np.asarray(ln0_g), "in_ln0_b": np.asarray(ln0_b),
        "in_w_tiles": w_tiles, "in_w_out": np.ascontiguousarray(np.asarray(w_out)[0]),
        "in_b_out": np.ascontiguousarray(np.asarray(b_out)[0]),
        "in_ln_g": np.ascontiguousarray(np.asarray(ln_g)[0]),
        "in_ln_b": np.ascontiguousarray(np.asarray(ln_b)[0]),
        "in_rel_bias": np.asarray(rel_bias),
        "in_onehot": bucket_onehot(), "in_selector": block_selector(), "in_mask": stick_mask(),
    }
    nc = bacc.Bacc("TRN2", target_bir_lowering=False, num_devices=1)
    args = [nc.dram_tensor(name, a.shape, mybir.dt.from_np(a.dtype), kind="ExternalInput").ap()
            for name, a in arrays.items()]
    out = nc.dram_tensor("out_dram", (T, D), F32, kind="ExternalOutput").ap()
    build(nc, *args, out)
    result = run_bass_kernel_spmd(nc, [arrays], core_ids=[0])
    return np.asarray(result.results[0]["out_dram"]).reshape(1, T, D)
```
